# Optimizing a Trainium2 kernel written in Bass

```python
import jax
import jax.numpy as jnp
from jax import lax
import numpy as np
import jax, jax.numpy as jnp

D_MODEL = 2048
BATCH = 1
SEQ = 256
DEPTH = 1

D_MIX = D_MODEL
D_RWKV = D_MIX // 2
RWKV_HEAD = 64
RWKV_HEADS = D_RWKV // RWKV_HEAD
D_POOL = D_MIX - D_RWKV
POOL_WINDOWS = (2, 4, 8, 16)
N_POOL_GROUPS = len(POOL_WINDOWS)
POOL_GROUP = D_POOL // N_POOL_GROUPS
DECAY_LORA = max(32, int(round(1.8 * D_RWKV ** 0.5 / 32)) * 32)
AAA_LORA = max(32, int(round(1.8 * D_RWKV ** 0.5 / 32)) * 32)
GATE_LORA = max(32, int(round(0.6 * D_RWKV ** 0.8 / 32)) * 32)
RWKV_SPLITS = (D_RWKV, 2 * D_RWKV, 3 * D_RWKV, 3 * D_RWKV + DECAY_LORA, 3 * D_RWKV + DECAY_LORA + AAA_LORA)
N_RWKV_COLS = 3 * D_RWKV + DECAY_LORA + AAA_LORA + GATE_LORA
D_IN = N_RWKV_COLS + D_POOL
D_FF = ((8 * D_MODEL // 3 + 255) // 256) * 256
CONV_WIDTH = 3
N_MOD = 6
RMS_EPS = 1e-6
GN_EPS = 64e-5
L2_EPS = 1e-12


def _rmsnorm(x, g):
    xf = x.astype(jnp.float32)
    y = xf * lax.rsqrt(jnp.mean(xf * xf, axis=-1, keepdims=True) + RMS_EPS)
    return (y * g.astype(jnp.float32)).astype(x.dtype)

def _token_shift(z):
    return jnp.pad(z, ((0, 0), (1, 0), (0, 0)))[:, :-1]

def _wkv7_scan(r, w, k, v, a, b):
    B, T, H, N = r.shape

    def step(S, inp):
        r_t, w_t, k_t, v_t, a_t, b_t = inp
        sa = jnp.einsum('bhvk,bhk->bhv', S, a_t)
        S = S * w_t[:, :, None, :] + sa[..., None] * b_t[:, :, None, :] + v_t[..., None] * k_t[:, :, None, :]
        y = jnp.einsum('bhvk,bhk->bhv', S, r_t)
        return S, y

    xs = (jnp.moveaxis(r, 1, 0), jnp.moveaxis(w, 1, 0), jnp.moveaxis(k, 1, 0),
          jnp.moveaxis(v, 1, 0), jnp.moveaxis(a, 1, 0), jnp.moveaxis(b, 1, 0))
    S0 = jnp.zeros((B, H, N, N), jnp.float32)
    _, ys = lax.scan(step, S0, xs)
    return jnp.moveaxis(ys, 0, 1)

def _rwkv7_mixer(p, mu, w0, w2, a0, a2, g2, k_k, k_a, r_k, ln_w, ln_b):
    B, T, _ = p.shape
    f32 = jnp.float32
    p = p + mu * (_token_shift(p) - p)
    r, k, v, xw, xa, xg = jnp.split(p, list(RWKV_SPLITS), axis=-1)
    w = -jax.nn.softplus(-(w0 + jnp.tanh(xw) @ w2)) - 0.5
    a = jax.nn.sigmoid(a0 + xa @ a2)
    g = jax.nn.sigmoid(xg) @ g2

    def heads(z):
        return z.reshape(B, T, RWKV_HEADS, RWKV_HEAD)

    kk = heads(k * k_k).astype(f32)
    kk = kk / jnp.maximum(jnp.sqrt(jnp.sum(kk * kk, axis=-1, keepdims=True)), L2_EPS)
    k = k * (1.0 + (a - 1.0) * k_a)
    r_h, k_h, v_h, a_h = heads(r), heads(k), heads(v), heads(a)
    decay = jnp.exp(-jnp.exp(heads(w).astype(f32)))
    y = _wkv7_scan(r_h.astype(f32), decay, k_h.astype(f32), v_h.astype(f32),
                   -kk, kk * a_h.astype(f32))
    mean = jnp.mean(y, axis=-1, keepdims=True)
    var = jnp.mean(jnp.square(y - mean), axis=-1, keepdims=True)
    y = ((y - mean) * lax.rsqrt(var + GN_EPS)).reshape(B, T, D_RWKV)
    y = (y * ln_w.astype(f32) + ln_b.astype(f32)).astype(p.dtype)
    bonus = jnp.sum(r_h * k_h * r_k, axis=-1, keepdims=True) * v_h
    return (y + bonus.reshape(B, T, D_RWKV)) * g

def _pool_mixer(u, pool_w, pool_b, pool_scale):
    B, T, _ = u.shape
    uf = u.astype(jnp.float32).reshape(B, T, N_POOL_GROUPS, POOL_GROUP)
    cs = jnp.cumsum(uf, axis=1)
    pos = jnp.arange(1, T + 1, dtype=jnp.float32)
    outs = []
    for gi, win in enumerate(POOL_WINDOWS):
        c_g = cs[:, :, gi]
        lag = jnp.pad(c_g, ((0, 0), (win, 0), (0, 0)))[:, :T]
        mean = (c_g - lag) / jnp.minimum(pos, win)[None, :, None]
        outs.append(mean - uf[:, :, gi])
    z = jnp.stack(outs, axis=2).astype(u.dtype)
    z = jnp.einsum('btgc,gcd->btgd', z, pool_w) + pool_b
    return z.reshape(B, T, D_POOL) * pool_scale

def _conv_ffn(h, w_up, conv_w, conv_b, w_down):
    T = h.shape[1]
    u = h @ w_up
    up = jnp.pad(u, ((0, 0), (CONV_WIDTH - 1, 0), (0, 0)))
    y = conv_b
    for j in range(CONV_WIDTH):
        y = y + conv_w[j] * up[:, j:j + T]
    val, gate = jnp.split(y, 2, axis=-1)
    return (jax.nn.silu(gate) * val) @ w_down

def first_inputs(seed: int = 0) -> dict:
    key = jax.random.key(seed)
    ks = jax.random.split(key, 27)
    L = DEPTH

    def nrm(k, shape, scale):
        return jax.random.normal(k, shape, jnp.float32) * scale

    ratio = jnp.arange(D_RWKV, dtype=jnp.float32) / (D_RWKV - 1)
    w0 = (-7.0 + 5.0 * ratio ** 0.85 + 0.5)[None, :] + nrm(ks[5], (L, D_RWKV), 0.1)
    return {
        'x': nrm(ks[0], (BATCH, SEQ, D_MODEL), 1.0),
        'c': nrm(ks[1], (BATCH, D_MODEL), 1.0),
        'w_ada': nrm(ks[2], (L, D_MODEL, N_MOD * D_MODEL), D_MODEL ** -0.5),
        'b_ada': nrm(ks[3], (L, N_MOD * D_MODEL), 0.01),
        'norm1_g': 1.0 + nrm(ks[4], (L, D_MODEL), 0.05),
        'w_in': nrm(ks[6], (L, D_MODEL, D_IN), D_MODEL ** -0.5),
        'mu_shift': jax.random.uniform(ks[7], (L, N_RWKV_COLS), jnp.float32),
        'w0': w0,
        'w2': nrm(ks[8], (L, DECAY_LORA, D_RWKV), 0.5 * DECAY_LORA ** -0.5),
        'a0': nrm(ks[9], (L, D_RWKV), 0.1),
        'a2': nrm(ks[10], (L, AAA_LORA, D_RWKV), AAA_LORA ** -0.5),
        'g2': nrm(ks[11], (L, GATE_LORA, D_RWKV), GATE_LORA ** -0.5),
        'k_k': 0.85 + nrm(ks[12], (L, D_RWKV), 0.05),
        'k_a': 1.0 + nrm(ks[13], (L, D_RWKV), 0.05),
        'r_k': nrm(ks[14], (L, RWKV_HEADS, RWKV_HEAD), 0.1),
        'ln_x_w': 1.0 + nrm(ks[15], (L, D_RWKV), 0.05),
        'ln_x_b': nrm(ks[16], (L, D_RWKV), 0.01),
        'pool_w': nrm(ks[17], (L, N_POOL_GROUPS, POOL_GROUP, POOL_GROUP), POOL_GROUP ** -0.5),
        'pool_b': nrm(ks[18], (L, N_POOL_GROUPS, POOL_GROUP), 0.01),
        'pool_scale': 1.0 + nrm(ks[19], (L, D_POOL), 0.05),
        'w_out': nrm(ks[20], (L, D_MIX, D_MODEL), D_MIX ** -0.5),
        'norm2_g': 1.0 + nrm(ks[21], (L, D_MODEL), 0.05),
        'w_up': nrm(ks[22], (L, D_MODEL, 2 * D_FF), D_MODEL ** -0.5),
        'conv_w': nrm(ks[23], (L, CONV_WIDTH, 2 * D_FF), CONV_WIDTH ** -0.5),
        'conv_b': nrm(ks[24], (L, 2 * D_FF), 0.01),
        'w_down': nrm(ks[25], (L, D_FF, D_MODEL), D_FF ** -0.5),
        'norm_f_g': 1.0 + nrm(ks[26], (D_MODEL,), 0.05),
    }

def first_block(x, c, w_ada, b_ada, norm1_g, w_in, mu_shift, w0, w2, a0, a2, g2,
              k_k, k_a, r_k, ln_x_w, ln_x_b, pool_w, pool_b, pool_scale, w_out,
              norm2_g, w_up, conv_w, conv_b, w_down, norm_f_g):
    c_act = jax.nn.silu(c)
    for l in range(DEPTH):
        mod = c_act @ w_ada[l] + b_ada[l]
        sh1, sc1, gt1, sh2, sc2, gt2 = jnp.split(mod[:, None, :], N_MOD, axis=-1)
        h = _rmsnorm(x, norm1_g[l]) * (1.0 + sc1) + sh1
        p = h @ w_in[l]
        y_rwkv = _rwkv7_mixer(p[..., :N_RWKV_COLS], mu_shift[l], w0[l], w2[l], a0[l], a2[l],
                              g2[l], k_k[l], k_a[l], r_k[l], ln_x_w[l], ln_x_b[l])
        y_pool = _pool_mixer(p[..., N_RWKV_COLS:], pool_w[l], pool_b[l], pool_scale[l])
        mix = jnp.concatenate([y_rwkv, y_pool], axis=-1) @ w_out[l]
        x = x + gt1 * mix
        h = _rmsnorm(x, norm2_g[l]) * (1.0 + sc2) + sh2
        x = x + gt2 * _conv_ffn(h, w_up[l], conv_w[l], conv_b[l], w_down[l])
    return _rmsnorm(x, norm_f_g)


ROPE_THETA = 500000.0
NORM_EPS = 1e-6
BLOCK = 128
MAX_POS_OFFSET = 1024

MLA_HEADS = D_MODEL // 128
MLA_NOPE = 128
MLA_ROPE = 64
MLA_V = 128
MLA_QK = MLA_NOPE + MLA_ROPE
MLA_KV_RANK = D_MODEL // 4
MLA_WIDTH = MLA_HEADS * MLA_V

DIL_GROUPS = ((128, 1), (512, 4), (2048, 16))
DIL_N_GROUPS = 3
DIL_HEADS = D_MODEL // 256
DIL_HEAD_DIM = 128
DIL_ROT = DIL_HEAD_DIM // 4
DIL_WIDTH = DIL_HEADS * DIL_HEAD_DIM
DIL_QKV = 3 * DIL_N_GROUPS * DIL_WIDTH

IN_SIZES = (MLA_HEADS * MLA_QK, MLA_KV_RANK + MLA_ROPE, MLA_WIDTH, DIL_QKV, DIL_WIDTH, D_MODEL, D_MODEL)
IN_SPLITS = (3072, 3648, 5696, 14912, 15936, 17984)
IN_TOTAL = 20032


def rms_norm(x, g):
    xf = x.astype(jnp.float32)
    y = xf * lax.rsqrt(jnp.mean(jnp.square(xf), axis=-1, keepdims=True) + NORM_EPS)
    return (y * g.astype(jnp.float32)).astype(x.dtype)

def rotary(x, positions):
    r = x.shape[-1]
    inv_freq = 1.0 / (ROPE_THETA ** (jnp.arange(0, r, 2, dtype=jnp.float32) / r))
    ang = positions.astype(jnp.float32)[:, :, None, None] * inv_freq
    cos, sin = jnp.cos(ang), jnp.sin(ang)
    xf = x.astype(jnp.float32)
    x1, x2 = xf[..., : r // 2], xf[..., r // 2:]
    return jnp.concatenate([x1 * cos - x2 * sin, x2 * cos + x1 * sin], axis=-1).astype(x.dtype)

def partial_rotary(x, positions):
    return jnp.concatenate([rotary(x[..., :DIL_ROT], positions), x[..., DIL_ROT:]], axis=-1)

def causal_dense_attention(q, k, v):
    B, S, H, Dk = q.shape
    n_blk = S // BLOCK
    scale = Dk ** -0.5
    qb = jnp.moveaxis(q.reshape(B, n_blk, BLOCK, H, Dk), 1, 0)
    k_pos = jnp.arange(S)

    def one_block(args):
        q_blk, blk = args
        s = jnp.einsum('bqhd,bkhd->bhqk', q_blk, k, preferred_element_type=jnp.float32) * scale
        q_pos = blk * BLOCK + jnp.arange(BLOCK)
        s = jnp.where(k_pos[None, :] <= q_pos[:, None], s, -jnp.inf)
        p = jax.nn.softmax(s, axis=-1)
        return jnp.einsum('bhqk,bkhd->bqhd', p.astype(v.dtype), v)

    out = lax.map(one_block, (qb, jnp.arange(n_blk)))
    return jnp.moveaxis(out, 0, 1).reshape(B, S, H, v.shape[-1])

def dilated_group_attention(q, k, v, window, dilation):
    B, S, H, D = q.shape
    n_steps = window // dilation
    span = dilation * BLOCK
    s_pad = -(-S // span) * span
    n_blk = s_pad // span

    def to_blocks(t):
        t = jnp.pad(t, ((0, 0), (0, s_pad - S), (0, 0), (0, 0)))
        t = jnp.swapaxes(t.reshape(B, s_pad // dilation, dilation, H, D), 1, 2)
        return t.reshape(B, dilation, n_blk, BLOCK, H, D)

    def with_prev(t):
        prev = jnp.pad(t[:, :, :-1], ((0, 0), (0, 0), (1, 0), (0, 0), (0, 0), (0, 0)))
        return jnp.concatenate([prev, t], axis=3)

    qb = to_blocks(q)
    kb = with_prev(to_blocks(k))
    vb = with_prev(to_blocks(v))
    s = jnp.einsum('brnqhd,brnkhd->brnhqk', qb, kb, preferred_element_type=jnp.float32) * (D ** -0.5)
    q_idx = BLOCK + jnp.arange(BLOCK)[:, None]
    k_idx = jnp.arange(2 * BLOCK)[None, :]
    rel = q_idx - k_idx
    band = (rel >= 0) & (rel <= n_steps)
    has_prev = (jnp.arange(n_blk) > 0)[:, None, None] | (k_idx >= BLOCK)[None]
    valid = band[None] & has_prev
    s = jnp.where(valid[None, None, :, None], s, -jnp.inf)
    m = jnp.max(s, axis=-1, keepdims=True)
    e = jnp.exp(s - m)
    l = jnp.sum(e, axis=-1, keepdims=True)
    o = jnp.einsum('brnhqk,brnkhd->brnqhd', (e / l).astype(v.dtype), vb)
    lse = jnp.swapaxes((m + jnp.log(l))[..., 0], 3, 4)

    def from_blocks(t):
        t = t.reshape((B, dilation, s_pad // dilation) + t.shape[4:])
        t = jnp.swapaxes(t, 1, 2)
        return t.reshape((B, s_pad) + t.shape[3:])[:, :S]

    return from_blocks(o), from_blocks(lse)

def mla_branch(q_all, kv_a, positions, g_kv, w_kv_b):
    B, S, _ = q_all.shape
    q = q_all.reshape(B, S, MLA_HEADS, MLA_QK)
    q = jnp.concatenate([q[..., :MLA_NOPE], rotary(q[..., MLA_NOPE:], positions)], axis=-1)
    c_kv = rms_norm(kv_a[..., :MLA_KV_RANK], g_kv)
    k_pe = rotary(kv_a[..., MLA_KV_RANK:][:, :, None, :], positions)
    kv = jnp.einsum('bsr,rhe->bshe', c_kv, w_kv_b.reshape(MLA_KV_RANK, MLA_HEADS, MLA_NOPE + MLA_V))
    k = jnp.concatenate([kv[..., :MLA_NOPE], jnp.broadcast_to(k_pe, (B, S, MLA_HEADS, MLA_ROPE))], axis=-1)
    v = kv[..., MLA_NOPE:]
    return causal_dense_attention(q, k, v).reshape(B, S, MLA_WIDTH)

def dilated_branch(qkv, positions):
    B, S, _ = qkv.shape
    qkv = qkv.reshape(B, S, 3, DIL_N_GROUPS * DIL_HEADS, DIL_HEAD_DIM)
    q = partial_rotary(qkv[:, :, 0], positions).reshape(B, S, DIL_N_GROUPS, DIL_HEADS, DIL_HEAD_DIM)
    k = partial_rotary(qkv[:, :, 1], positions).reshape(B, S, DIL_N_GROUPS, DIL_HEADS, DIL_HEAD_DIM)
    v = qkv[:, :, 2].reshape(B, S, DIL_N_GROUPS, DIL_HEADS, DIL_HEAD_DIM)
    outs, lses = [], []
    for g, (window, dilation) in enumerate(DIL_GROUPS):
        o, lse = dilated_group_attention(q[:, :, g], k[:, :, g], v[:, :, g], window, dilation)
        outs.append(o)
        lses.append(lse)
    wts = jax.nn.softmax(jnp.stack(lses, axis=0), axis=0)
    o = jnp.sum(wts[..., None] * jnp.stack(outs, axis=0).astype(jnp.float32), axis=0)
    return o.astype(qkv.dtype).reshape(B, S, DIL_WIDTH)

def second_inputs(seed: int = 0) -> dict:
    key = jax.random.key(seed)
    ks = jax.random.split(key, 16)

    def nrm(k, shape, fan_in):
        return jax.random.normal(k, shape, jnp.float32) * (fan_in ** -0.5)

    x = jax.random.normal(ks[0], (BATCH, SEQ, D_MODEL), jnp.float32)
    c = jax.random.normal(ks[1], (BATCH, D_MODEL), jnp.float32)
    offset = jax.random.randint(ks[2], (BATCH, 1), 0, MAX_POS_OFFSET, dtype=jnp.int32)
    positions = jnp.arange(SEQ, dtype=jnp.int32)[None, :] + offset
    w_ada = nrm(ks[3], (DEPTH, D_MODEL, 3 * D_MODEL), D_MODEL)
    b_ada = 0.02 * jax.random.normal(ks[4], (DEPTH, 3 * D_MODEL), jnp.float32)
    g_pre = 1.0 + 0.02 * jax.random.normal(ks[5], (DEPTH, D_MODEL), jnp.float32)
    g_post = 1.0 + 0.02 * jax.random.normal(ks[6], (DEPTH, D_MODEL), jnp.float32)
    w_in = nrm(ks[7], (DEPTH, D_MODEL, IN_TOTAL), D_MODEL)
    g_kv = 1.0 + 0.02 * jax.random.normal(ks[8], (DEPTH, MLA_KV_RANK), jnp.float32)
    w_kv_b = nrm(ks[9], (DEPTH, MLA_KV_RANK, MLA_HEADS * (MLA_NOPE + MLA_V)), MLA_KV_RANK)
    w_mla_proj = nrm(ks[10], (DEPTH, MLA_WIDTH, D_MODEL), MLA_WIDTH)
    w_dil_proj = nrm(ks[11], (DEPTH, DIL_WIDTH, D_MODEL), DIL_WIDTH)
    w_o = nrm(ks[12], (DEPTH, D_MODEL, D_MODEL), D_MODEL)
    return {'x': x, 'c': c, 'positions': positions, 'w_ada': w_ada, 'b_ada': b_ada,
            'g_pre': g_pre, 'g_post': g_post, 'w_in': w_in, 'g_kv': g_kv, 'w_kv_b': w_kv_b,
            'w_mla_proj': w_mla_proj, 'w_dil_proj': w_dil_proj, 'w_o': w_o}

def second_block(x, c, positions, w_ada, b_ada, g_pre, g_post, w_in, g_kv, w_kv_b,
              w_mla_proj, w_dil_proj, w_o):
    for layer in range(DEPTH):
        mod = jnp.einsum('bd,de->be', jax.nn.silu(c), w_ada[layer]) + b_ada[layer]
        shift, scale, gate = jnp.split(mod, 3, axis=-1)
        h = rms_norm(x, g_pre[layer]) * (1.0 + scale[:, None, :]) + shift[:, None, :]
        proj = jnp.einsum('bsd,de->bse', h, w_in[layer])
        q_mla, kv_a, z_mla, qkv_dil, z_dil, gl_mla, gl_dil = jnp.split(proj, IN_SPLITS, axis=-1)
        a = mla_branch(q_mla, kv_a, positions, g_kv[layer], w_kv_b[layer]) * jax.nn.silu(z_mla)
        y_mla = jnp.einsum('bse,ed->bsd', a, w_mla_proj[layer])
        bb = dilated_branch(qkv_dil, positions) * jax.nn.silu(z_dil)
        y_dil = jnp.einsum('bse,ed->bsd', bb, w_dil_proj[layer])
        merged = jax.nn.sigmoid(gl_mla) * y_mla + jax.nn.sigmoid(gl_dil) * y_dil
        out = jnp.einsum('bsd,de->bse', merged, w_o[layer])
        x = x + gate[:, None, :] * rms_norm(out, g_post[layer])
    return x


def setup_inputs(seed=0):
    out = dict(first_inputs(seed))
    for name, value in second_inputs(seed + 1).items():
        if name != "x":
            out[name + "_2"] = value
    return out


def reference(
    x, c, w_ada, b_ada, norm1_g, w_in, mu_shift, w0, w2, a0, a2, g2, k_k, k_a, r_k, ln_x_w,
    ln_x_b, pool_w, pool_b, pool_scale, w_out, norm2_g, w_up, conv_w, conv_b, w_down, norm_f_g,
    c_2, positions_2, w_ada_2, b_ada_2, g_pre_2, g_post_2, w_in_2, g_kv_2, w_kv_b_2,
    w_mla_proj_2, w_dil_proj_2, w_o_2,
):
    x = first_block(
        x, c, w_ada, b_ada, norm1_g, w_in, mu_shift, w0, w2, a0, a2, g2, k_k, k_a, r_k, ln_x_w,
        ln_x_b, pool_w, pool_b, pool_scale, w_out, norm2_g, w_up, conv_w, conv_b, w_down,
        norm_f_g,
    )
    return second_block(
        x, c_2, positions_2, w_ada_2, b_ada_2, g_pre_2, g_post_2, w_in_2, g_kv_2, w_kv_b_2,
        w_mla_proj_2, w_dil_proj_2, w_o_2,
    )


_drawn_inputs = setup_inputs


def setup_inputs(seed=0):
    import zlib

    import numpy as np

    out = dict(_drawn_inputs(seed))
    spreads = {}
    factors = {'b_ada': 3.097,
     'w2': 2.704,
     'a0': 4.572,
     'ln_x_w': 4.393,
     'ln_x_b': 8.0,
     'pool_b': 8.0,
     'conv_b': 8.0,
     'g_pre_2': 4.044,
     'g_post_2': 5.399,
     'g_kv_2': 8.0}
    for name, (base, spread) in spreads.items():
        noise = np.random.default_rng([zlib.crc32(name.encode()), seed]).standard_normal(out[name].shape)
        drawn = base * np.exp(spread * noise) if base else spread * noise
        out[name] = jnp.asarray(drawn.astype(out[name].dtype))
    for name, factor in factors.items():
        out[name] = (out[name] * factor).astype(out[name].dtype)
    return out
```

```python
from contextlib import ExitStack

import concourse.bass as bass
from concourse import mybir

F32 = mybir.dt.float32
F32R = mybir.dt.float32r
I32 = mybir.dt.int32
ACT = mybir.ActivationFunctionType
ALU = mybir.AluOpType
AX = mybir.AxisListType

P = 128
T = 256
D = 2048
DT = D // P
RT = 8
CH = 64
DECAY = 0.6065306597126334
KB = 1024
BASE = 16512

C_ONES, C_ID, C_BLK, C_MU, C_LOW, C_LOWT, C_INVC = 0, 128, 256, 384, 640, 1408, 2176
C_WKV = 2240
C_ATT = 4 * 384
LEVELS = (1, 2, 4, 8, 16, 32)
WINDOWS = (2, 4, 8, 16)

PAR = {}
for _name, _n in (("c", 16), ("c_2", 16), ("b_ada", 144), ("norm1_g", 16), ("mu", 27), ("w0", 8), ("a0", 8),
                  ("k_k", 8), ("k_a", 8), ("r_k", 8), ("ln_w", 8), ("ln_b", 8), ("pool_b", 8), ("pool_s", 8),
                  ("norm2_g", 16), ("conv", 88 * 3), ("conv_b", 88), ("norm_f", 16), ("g_pre", 16),
                  ("g_post", 16), ("g_kv", 4), ("freq", 4)):
    PAR[_name] = (sum(n for _, n in PAR.values()), _n)
N_PAR = sum(n for _, n in PAR.values())

LOOP_STEPS = {
        ("sp", "ada0"): {"w_free0": 1, "w_free1": 1, "w_free2": 1, "w_free3": 1},
        ("sp", "rkv"): {"w_free0": 1, "w_free1": 1, "w_free2": 1, "w_free3": 1},
        ("sp", "ada1"): {"w_free0": 1, "w_free1": 1, "w_free2": 1, "w_free3": 1},
        ("sp", "w_out"): {"w_free0": 1, "w_free1": 1, "w_free2": 1, "w_free3": 1},
        ("sp", "ffn_a"): {"w_free0": 4, "w_free1": 4, "w_free2": 4, "w_free3": 4},
        ("sp", "ffn_b"): {"w_free0": 4, "w_free1": 4, "w_free2": 4, "w_free3": 4},
        ("sp", "mla0"): {"w_free0": 2, "w_free1": 2, "w_free2": 2, "w_free3": 2},
        ("sp", "proj0"): {"w_free0": 1, "w_free1": 1, "w_free2": 1, "w_free3": 1},
        ("sp", "mla1"): {"w_free0": 2, "w_free1": 2, "w_free2": 2, "w_free3": 2},
        ("sp", "proj1"): {"w_free0": 1, "w_free1": 1, "w_free2": 1, "w_free3": 1},
        ("sp", "gl"): {"w_free0": 1, "w_free1": 1, "w_free2": 1, "w_free3": 1},
        ("sp", "dil"): {"w_free0": 3, "w_free1": 3, "w_free2": 3, "w_free3": 3},
        ("sp", "dproj"): {"w_free0": 1, "w_free1": 1, "w_free2": 1, "w_free3": 1},
        ("sp", "w_o"): {"w_free0": 1, "w_free1": 1, "w_free2": 1, "w_free3": 1},
        ("pool", "ffn_a"): {"w_landed0": 64, "w_landed1": 64, "w_landed2": 64, "w_landed3": 64, "ada_full": 1,
        "pool_seq": 31},
        ("pool", "ffn_b"): {"w_landed0": 64, "w_landed1": 64, "w_landed2": 64, "w_landed3": 64, "ada_full": 1,
        "pool_seq": 31},
        ("pool", "mla0"): {"w_landed0": 32, "w_landed1": 48, "w_landed2": 32, "w_landed3": 32, "ada_full": 1,
        "pool_seq": 31},
        ("pool", "mla1"): {"w_landed0": 32, "w_landed1": 48, "w_landed2": 32, "w_landed3": 32, "ada_full": 1,
        "pool_seq": 31},
        ("pe", "ada0"): {"w_landed0": 16, "w_free0": 1, "w_landed1": 16, "w_free1": 1, "w_landed2": 16,
        "w_free2": 1, "w_landed3": 16, "w_free3": 1, "ada_sums": 1, "ada_free": 1},
        ("pe", "rkv"): {"w_landed0": 16, "w_free0": 1, "w_landed1": 16, "w_free1": 1, "w_landed2": 16,
        "w_free2": 1, "w_landed3": 16, "w_free3": 1, "bank_free0": 1, "bank_free1": 1, "bank_free2": 1,
        "bank_free3": 1},
        ("pe", "ada1"): {"w_landed0": 16, "w_free0": 1, "w_landed1": 16, "w_free1": 1, "w_landed2": 16,
        "w_free2": 1, "w_landed3": 16, "w_free3": 1, "ada_sums": 1, "ada_free": 1},
        ("pe", "w_out"): {"w_landed0": 16, "w_free0": 1, "w_landed1": 16, "w_free1": 1, "w_landed2": 16,
        "w_free2": 1, "w_landed3": 16, "w_free3": 1, "bank_free0": 1, "bank_free1": 1, "bank_free2": 1,
        "bank_free3": 1},
        ("pe", "ffn_a"): {"x_free4": 2, "w_landed0": 64, "w_free0": 4, "w_landed1": 64, "w_free1": 4,
        "w_landed2": 64, "w_free2": 4, "w_landed3": 64, "w_free3": 4, "ada_sums": 1, "ada_free": 1, "dve_to_pe":
        2, "bank_free0": 3, "bank_free1": 3, "bank_free2": 3, "x_free5": 2, "bank_free3": 3},
        ("pe", "ffn_b"): {"x_free4": 2, "w_landed0": 64, "w_free0": 4, "w_landed1": 64, "w_free1": 4,
        "w_landed2": 64, "w_free2": 4, "w_landed3": 64, "w_free3": 4, "ada_sums": 1, "ada_free": 1, "dve_to_pe":
        2, "bank_free0": 3, "bank_free1": 3, "bank_free2": 3, "x_free5": 2, "bank_free3": 3},
        ("pe", "mla0"): {"x_free4": 2, "x_full": 5, "w_landed0": 32, "w_free0": 2, "w_landed1": 48, "w_free1":
        2, "w_landed2": 32, "w_free2": 2, "w_landed3": 32, "w_free3": 2, "ada_sums": 1, "ada_free": 1,
        "dve_to_pe": 3, "bank_free0": 2, "bank_free1": 2, "bank_free2": 1, "x_free5": 2, "x_free7": 2,
        "bank_free3": 1},
        ("pe", "proj0"): {"w_landed0": 16, "w_free0": 1, "w_landed1": 16, "w_free1": 1, "w_landed2": 16,
        "w_free2": 1, "w_landed3": 16, "w_free3": 1, "bank_free0": 1, "bank_free1": 1, "bank_free2": 1,
        "bank_free3": 1},
        ("pe", "mla1"): {"x_free4": 2, "x_full": 5, "w_landed0": 32, "w_free0": 2, "w_landed1": 48, "w_free1":
        2, "w_landed2": 32, "w_free2": 2, "w_landed3": 32, "w_free3": 2, "ada_sums": 1, "ada_free": 1,
        "dve_to_pe": 3, "bank_free0": 2, "bank_free1": 2, "bank_free2": 1, "x_free5": 2, "x_free7": 2,
        "bank_free3": 1},
        ("pe", "proj1"): {"w_landed0": 16, "w_free0": 1, "w_landed1": 16, "w_free1": 1, "w_landed2": 16,
        "w_free2": 1, "w_landed3": 16, "w_free3": 1, "bank_free0": 1, "bank_free1": 1, "bank_free2": 1,
        "bank_free3": 1},
        ("pe", "gl"): {"w_landed0": 16, "w_free0": 1, "w_landed1": 16, "w_free1": 1, "w_landed2": 16, "w_free2":
        1, "w_landed3": 16, "w_free3": 1, "bank_free0": 1, "bank_free1": 1, "bank_free2": 1, "bank_free3": 1},
        ("pe", "dil"): {"x_free4": 3, "x_full": 7, "w_landed0": 48, "w_free0": 3, "w_landed1": 48, "w_free1": 3,
        "w_landed2": 48, "w_free2": 3, "w_landed3": 48, "w_free3": 3, "dve_to_pe": 2, "bank_free0": 3,
        "bank_free1": 3, "bank_free2": 3, "x_free5": 2, "x_free7": 2, "bank_free3": 3},
        ("pe", "dproj"): {"w_landed0": 16, "w_free0": 1, "w_landed1": 16, "w_free1": 1, "w_landed2": 16,
        "w_free2": 1, "w_landed3": 16, "w_free3": 1, "bank_free0": 1, "bank_free1": 1, "bank_free2": 1,
        "bank_free3": 1},
        ("pe", "w_o"): {"w_landed0": 16, "w_free0": 1, "w_landed1": 16, "w_free1": 1, "w_landed2": 16,
        "w_free2": 1, "w_landed3": 16, "w_free3": 1, "bank_free0": 1, "bank_free1": 1, "bank_free2": 1,
        "bank_free3": 1},
        ("act", "rkv"): {"w_landed0": 16, "w_landed1": 16, "w_landed2": 16, "w_landed3": 16, "high_done": 4,
        "unit_done": 4, "raw_free": 4},
        ("act", "w_out"): {"w_landed0": 16, "w_landed1": 16, "w_landed2": 16, "w_landed3": 16, "high_done": 4,
        "unit_done": 4},
        ("act", "ffn_a"): {"dve_to_act": 8, "w_landed0": 64, "w_landed1": 64, "w_landed2": 64, "w_landed3": 64,
        "high_done": 12, "unit_done": 12, "raw_free": 8},
        ("act", "ffn_b"): {"dve_to_act": 8, "w_landed0": 64, "w_landed1": 64, "w_landed2": 64, "w_landed3": 64,
        "high_done": 12, "unit_done": 12, "raw_free": 8},
        ("act", "mla0"): {"dve_to_act": 3, "x_full": 5, "w_landed0": 32, "w_landed1": 48, "w_landed2": 32,
        "w_landed3": 32, "high_done": 6, "unit_done": 6},
        ("act", "proj0"): {"w_landed0": 16, "w_landed1": 16, "w_landed2": 16, "w_landed3": 16, "high_done": 4,
        "unit_done": 4},
        ("act", "mla1"): {"dve_to_act": 3, "x_full": 5, "w_landed0": 32, "w_landed1": 48, "w_landed2": 32,
        "w_landed3": 32, "high_done": 6, "unit_done": 6},
        ("act", "proj1"): {"w_landed0": 16, "w_landed1": 16, "w_landed2": 16, "w_landed3": 16, "high_done": 4,
        "unit_done": 4},
        ("act", "gl"): {"w_landed0": 16, "w_landed1": 16, "w_landed2": 16, "w_landed3": 16, "high_done": 4,
        "unit_done": 4},
        ("act", "dil"): {"dve_to_act": 2, "x_full": 7, "w_landed0": 48, "w_landed1": 48, "w_landed2": 48,
        "w_landed3": 48, "high_done": 12, "unit_done": 12},
        ("act", "dproj"): {"w_landed0": 16, "w_landed1": 16, "w_landed2": 16, "w_landed3": 16, "high_done": 4,
        "unit_done": 4},
        ("act", "w_o"): {"w_landed0": 16, "w_landed1": 16, "w_landed2": 16, "w_landed3": 16, "high_done": 4,
        "unit_done": 4},
        ("dve", "ada0"): {"dve_seq": 12, "w_landed0": 16, "w_free0": 1, "w_landed1": 16, "w_free1": 1,
        "w_landed2": 16, "w_free2": 1, "w_landed3": 16, "w_free3": 1, "ada_full": 1},
        ("dve", "rkv"): {"dve_seq": 4, "w_landed0": 16, "w_free0": 1, "w_landed1": 16, "w_free1": 1,
        "w_landed2": 16, "w_free2": 1, "w_landed3": 16, "w_free3": 1, "high_done": 4, "bank_free0": 1,
        "bank_free1": 1, "bank_free2": 1, "bank_free3": 1, "raw_free": 4},
        ("dve", "ada1"): {"dve_seq": 12, "w_landed0": 16, "w_free0": 1, "w_landed1": 16, "w_free1": 1,
        "w_landed2": 16, "w_free2": 1, "w_landed3": 16, "w_free3": 1, "ada_full": 1},
        ("dve", "w_out"): {"w_landed0": 16, "w_free0": 1, "w_landed1": 16, "w_free1": 1, "w_landed2": 16,
        "w_free2": 1, "w_landed3": 16, "w_free3": 1, "high_done": 4, "bank_free0": 1, "bank_free1": 1,
        "bank_free2": 1, "bank_free3": 1, "unit_done": 4},
        ("dve", "ffn_a"): {"dve_seq": 22, "x_free4": 2, "act_to_dve": 8, "w_landed0": 64, "w_free0": 4,
        "w_landed1": 64, "w_free1": 4, "w_landed2": 64, "w_free2": 4, "w_landed3": 64, "w_free3": 4, "ada_full":
        1, "high_done": 12, "bank_free0": 3, "bank_free1": 3, "bank_free2": 3, "x_free5": 2, "bank_free3": 3,
        "raw_free": 8, "unit_done": 12, "dve_to_pe": 2},
        ("dve", "ffn_b"): {"dve_seq": 22, "x_free4": 2, "act_to_dve": 8, "w_landed0": 64, "w_free0": 4,
        "w_landed1": 64, "w_free1": 4, "w_landed2": 64, "w_free2": 4, "w_landed3": 64, "w_free3": 4, "ada_full":
        1, "high_done": 12, "bank_free0": 3, "bank_free1": 3, "bank_free2": 3, "x_free5": 2, "bank_free3": 3,
        "raw_free": 8, "unit_done": 12, "dve_to_pe": 2},
        ("dve", "mla0"): {"dve_seq": 9, "x_free4": 2, "x_full": 5, "act_to_dve": 5, "w_landed0": 32, "w_free0":
        2, "w_landed1": 48, "w_free1": 2, "w_landed2": 32, "w_free2": 2, "w_landed3": 32, "w_free3": 2,
        "ada_full": 1, "high_done": 6, "bank_free0": 2, "bank_free1": 2, "bank_free2": 1, "x_free5": 2,
        "x_free7": 2, "bank_free3": 1, "unit_done": 6},
        ("dve", "proj0"): {"w_landed0": 16, "w_free0": 1, "w_landed1": 16, "w_free1": 1, "w_landed2": 16,
        "w_free2": 1, "w_landed3": 16, "w_free3": 1, "high_done": 4, "bank_free0": 1, "bank_free1": 1,
        "bank_free2": 1, "bank_free3": 1, "unit_done": 4},
        ("dve", "mla1"): {"dve_seq": 9, "x_free4": 2, "x_full": 5, "act_to_dve": 5, "w_landed0": 32, "w_free0":
        2, "w_landed1": 48, "w_free1": 2, "w_landed2": 32, "w_free2": 2, "w_landed3": 32, "w_free3": 2,
        "ada_full": 1, "high_done": 6, "bank_free0": 2, "bank_free1": 2, "bank_free2": 1, "x_free5": 2,
        "x_free7": 2, "bank_free3": 1, "unit_done": 6},
        ("dve", "proj1"): {"w_landed0": 16, "w_free0": 1, "w_landed1": 16, "w_free1": 1, "w_landed2": 16,
        "w_free2": 1, "w_landed3": 16, "w_free3": 1, "high_done": 4, "bank_free0": 1, "bank_free1": 1,
        "bank_free2": 1, "bank_free3": 1, "unit_done": 4},
        ("dve", "gl"): {"dve_seq": 4, "w_landed0": 16, "w_free0": 1, "w_landed1": 16, "w_free1": 1, "w_landed2":
        16, "w_free2": 1, "w_landed3": 16, "w_free3": 1, "high_done": 4, "bank_free0": 1, "bank_free1": 1,
        "bank_free2": 1, "bank_free3": 1},
        ("dve", "dil"): {"dve_seq": 30, "x_free4": 3, "x_full": 7, "act_to_dve": 3, "w_landed0": 48, "w_free0":
        3, "w_landed1": 48, "w_free1": 3, "w_landed2": 48, "w_free2": 3, "w_landed3": 48, "w_free3": 3,
        "high_done": 12, "bank_free0": 3, "bank_free1": 3, "bank_free2": 3, "x_free5": 2, "x_free7": 2,
        "bank_free3": 3, "unit_done": 12},
        ("dve", "dproj"): {"dve_seq": 4, "w_landed0": 16, "w_free0": 1, "w_landed1": 16, "w_free1": 1,
        "w_landed2": 16, "w_free2": 1, "w_landed3": 16, "w_free3": 1, "high_done": 4, "bank_free0": 1,
        "bank_free1": 1, "bank_free2": 1, "bank_free3": 1, "unit_done": 4},
        ("dve", "w_o"): {"w_landed0": 16, "w_free0": 1, "w_landed1": 16, "w_free1": 1, "w_landed2": 16,
        "w_free2": 1, "w_landed3": 16, "w_free3": 1, "high_done": 4, "bank_free0": 1, "bank_free1": 1,
        "bank_free2": 1, "bank_free3": 1},
}
LEARNED = {}


class Book:

    def __init__(self, engine):
        self.engine, self.n, self.loop = engine, {}, None

    def up(self, name, k=1):
        self.n[name] = self.n.get(name, 0) + k
        return self.at(name)

    def at(self, name, back=0):
        n = self.n.get(name, 0) - back
        if self.loop is None:
            return n
        step = self.loop[2].get(name, 0)
        return n + self.loop[1] * step if step else n

    def turns(self, eng, name, count, body):
        steps = LOOP_STEPS.get((self.engine, name), {})
        before = dict(self.n)
        with eng.Fori(0, count) as i:
            self.loop = (name, i, steps)
            body(i)
        self.loop = None
        real = {k: v - before.get(k, 0) for k, v in self.n.items() if v != before.get(k, 0)}
        LEARNED[(self.engine, name)] = real
        for k, v in real.items():
            self.n[k] = before.get(k, 0) + v * count


def program(nc, xT_in, consts, att_consts, params, pos, w_ada, w_in, w2, a2, g2, pool_w, w_out, w_up, w_down,
            w_ada2, w_in2, w_kvb, w_mla, w_dil, w_o, out):
    ctx = ExitStack()
    with ctx:
        ctx.enter_context(nc.sbuf_tensor("arena", [P, (229344 - 16512) // 4 - 8], F32))

        def at(name, kb, shape, dt=F32):
            return nc.alloc_sbuf_tensor_at(name, shape, dt, offset=BASE + int(kb * KB))

        def sem(name):
            return ctx.enter_context(nc.semaphore(name))

        def sems(name, n):
            return [sem(f"{name}{k}") for k in range(n)]

        xT = at("xT", 0, [P, DT, T])
        ring = [at(f"ring{s}", 16 + 8 * s, [P, 2048]) for s in range(4)]
        WH = [at(f"w_high{b}", 48 + 16 * b, [P, 2048], F32R) for b in range(2)]
        WL = [at(f"w_low{b}", 56 + 16 * b, [P, 2048], F32R) for b in range(2)]
        con = at("con", 80, [P, C_WKV])
        par = at("par", 89, [P, N_PAR])
        mod = at("mod", 92.5, [P, 9 * DT])
        cact = at("cact", 93.25, [P, 32])
        small = at("small", 93.5, [P, 64])
        eps = at("eps", 93.75, [P, 4])
        pc = at("pc", 94, [P, RT, 4])
        gs = at("gs", 94.25, [P, DT])
        post = at("post", 94.75, [P, T], I32)

        W0 = 96
        AH = at("act_high", W0, [P, DT, T], F32R)
        AL = at("act_low", W0 + 16, [P, DT, T], F32R)
        rkv = at("rkv", W0 + 32, [P, 24, T])
        aa = at("aa", W0 + 56, [P, RT, T])
        gg = at("gg", W0 + 64, [P, RT, T])
        sg = at("sg", W0 + 72, [P, RT, T])
        yp = at("yp", W0 + 80, [P, RT, T])
        zp = at("zp", W0 + 88, [P, RT, T])
        w2a2 = at("w2a2", W0 + 96, [P, 1024])
        g2a = at("g2a", W0 + 100, [P, 1024])
        g2b = at("g2b", W0 + 104, [P, 1024])
        pwt = at("pwt", W0 + 96, [P, 4, 2, T])
        tw = at("tw", W0 + 88, [P, T])
        ta = at("ta", W0 + 89, [P, T])
        tg = at("tg", W0 + 90, [P, T])
        tg2 = at("tg2", W0 + 91, [P, T])
        raw = [at(f"raw{b}", W0 + 108 + 1.125 * b, [P, 272]) for b in range(2)]
        dsh = at("dsh", W0 + 110.25, [P, T])
        pa = [at(f"pa{b}", W0 + 104 + 1.125 * b, [P, 272]) for b in range(2)]
        AR = at("AR", W0, [P, RT, 2, 2, P])
        Bt = at("Bt", W0 + 16, [P, RT, T])
        Kt = at("Kt", W0 + 24, [P, RT, T])
        kkn = at("kkn", 48, [P, RT, T])
        tmp1 = at("tmp1", 56, [P, RT, T])
        csum = at("csum", 64, [P, RT, T])
        ex = at("ex", 72, [P, RT, T])
        tmp2 = at("tmp2", W0 + 88, [P, RT, T])
        scanm = at("scanm", W0 + 96, [P, RT, T])
        bon = at("bon", W0 + 32, [P, RT, T])
        M24 = at("M24", 48, [P, 8, 2, P])
        M35 = at("M35", 56, [P, 8, 2, P])
        X = [at(f"X{b}", 64 + 2 * b, [P, 4, P]) for b in range(2)]
        XT = [at(f"XT{b}", 68 + 2 * b, [P, 4, P]) for b in range(2)]
        T1 = [at(f"T1{b}", 72 + 2 * b, [P, 4, P]) for b in range(2)]
        BZ = [at(f"BZ{c}", W0 + 88 + 2 * c, [P, 4, P]) for c in range(2)]
        KZ = [at(f"KZ{c}", W0 + 92 + 2 * c, [P, 4, P]) for c in range(2)]
        UP = at("UP", W0 + 96, [P, 4, 2, P])
        VP = at("VP", W0 + 100, [P, 4, 2, P])
        Z1 = at("Z1", W0 + 104, [P, 4, P])
        stmp = at("stmp", W0 + 106, [P, 4, P])
        S = [at(f"S{g}", W0 + 56 + 2 * g, [P, 4, P]) for g in range(2)]
        pcbd = at("pcbd", W0 + 60, [P, 4, P])
        sq = at("sq", W0 + 72, [P, DT, T])
        rstd = at("rstd", W0 + 88, [P, T])
        hf = at("hf", W0 + 90, [P, DT, T])
        HH = at("hid_high", W0 + 32, [P, 4, T], F32R)
        HL = at("hid_low", W0 + 36, [P, 4, T], F32R)
        dacc = at("dacc", W0 + 40, [P, DT, T])
        rawu = [at(f"rawu{b}", W0 + 56 + 1.125 * b, [P, T + 2]) for b in range(4)]
        cva = [at(f"cva{b}", W0 + 61 + b, [P, T]) for b in range(4)]
        sil = at("sil", W0 + 66, [P, T])
        hfu = at("hfu", W0 + 67, [P, T])
        acc0 = at("acc0", W0 + 32, [P, 512])
        acc1 = at("acc1", W0, [P, 512])
        acc2 = at("acc2", W0 + 68, [P, 512])
        prod2 = at("prod2", W0 + 70, [P, 512])
        prod3 = at("prod3", W0 + 99, [P, T])
        acc3 = at("acc3", W0 + 85, [P, T])
        BH = at("mix_high", W0 + 32, [P, 8, T], F32R)
        BL = at("mix_low", W0 + 40, [P, 8, T], F32R)
        Y = at("Y", W0 + 48, [P, DT, T])
        CKH = at("ckv_high", W0 + 64, [P, 4, T], F32R)
        CKL = at("ckv_low", W0 + 68, [P, 4, T], F32R)
        sgl = at("sgl", W0 + 64, [P, DT, T])
        ktn = at("ktn", W0 + 72, [P, 2, T])
        vv = at("vv", W0 + 74, [P, 2, 2, P])
        qn = at("qn", W0 + 76, [P, 2, T])
        qr = at("qr", W0 + 78, [P, T])
        kpe = at("kpe", W0 + 79, [P, T])
        cosM = at("cosM", W0 + 80, [P, T])
        sinM = at("sinM", W0 + 81, [P, T])
        cosD = at("cosD", W0 + 82, [P, T])
        sinD = at("sinD", W0 + 83, [P, T])
        rsw = at("rsw", W0 + 84, [P, T])
        rtm = at("rtm", W0 + 85, [P, T])
        Pr = at("Pr", W0 + 86, [P, 3, 384])
        PT = at("PT", W0 + 90.5, [P, 3, 384])
        zs = at("zs", W0 + 95, [P, 2, T])
        ez = at("ez", W0 + 97, [P, 2, T])
        af = at("af", W0 + 109, [P, 2, T])
        kd = at("kd", W0 + 100, [P, 3, T])
        qd = at("qd", W0 + 103, [P, 3, T])
        vd = at("vd", W0 + 106, [P, 3, 2, P])
        ckv = at("ckv", W0 + 100, [P, 4, T])
        cksq = at("cksq", W0 + 104, [P, 4, T])
        ang = at("ang", W0 + 100, [P, 2, T])
        tang = at("tang", W0 + 102, [P, 2, T])
        tred = at("tred", W0 + 104, [P, 2, T])
        posf = at("posf", W0 + 106, [P, T])
        oo = at("oo", W0 + 64, [P, DT, T])
        sqf = at("sqf", W0 + 80, [P, DT, T])
        rstf = at("rstf", W0 + 96, [P, T])

        bank = [ctx.enter_context(nc.psum_tensor(f"bank{b}", [P, 512], F32)) for b in range(8)]

        def cc(start, n=P):
            return con[:, start:start + n]

        def flat(t):
            return t[:, :, :].rearrange("p a b -> p (a b)")

        def pr(name, k=0, n=1):
            return par[:, PAR[name][0] + k:PAR[name][0] + k + n]

        inputs_landed = sem("inputs_landed")
        extra_landed = sem("extra_landed")
        w_landed = sems("w_landed", 4)
        w_free = sems("w_free", 4)
        high_done = sem("high_done")
        unit_done = sem("unit_done")
        bank_free = sems("bank_free", 4)
        x_full = sem("x_full")
        x_free = {b: sem(f"x_free{b}") for b in (4, 5, 7)}
        ada_sums = sem("ada_sums")
        pool_seq = sem("pool_seq")
        pool_spare = sem("pool_spare")
        ada_full = sem("ada_full")
        ada_free = sem("ada_free")
        raw_free = sem("raw_free")
        mix_ready = sem("mix_ready")
        act_seq = sem("act_seq")
        dve_seq = sem("dve_seq")
        act_to_dve = sem("act_to_dve")
        dve_to_act = sem("dve_to_act")
        act_to_pe = sem("act_to_pe")
        gate_pool = sem("gate_pool")
        dve_to_pe = sem("dve_to_pe")
        k_full = sem("k_full")
        k_free = sems("k_free", 7)
        gate_pe = sem("gate_pe")
        out_landed = sem("out_landed")
        spare = sem("spare")

        block = ctx.enter_context(nc.Block())

        XB = (4, 5, 7)
        UP_SLOT, ADA_SLOT = (0, 1, 3, 0, 2, 3, 1, 2), (2, 1, 0, 3)

        K_BANK, NK = (0, 1, 2, 3, 4, 5, 7), 7
        uses, use_of = [], {}

        def use(*key):
            use_of[key] = len(uses)
            uses.append(key)

        ITS = [(tt, hg) for tt in range(2) for hg in range(2)]
        for k in range(4):
            use("kk", k)
        for k in range(4):
            use("bonus", k)
        for it in range(4):
            for w in "BKV":
                use(it, "tr", w)
            for hb in range(2):
                use(it, "M1", hb)
            for k in range(2):
                for hb in range(2):
                    use(it, "M24", hb, k)
                    use(it, "M35", hb, k)
            for n in LEVELS[1:]:
                for hb in range(2):
                    use(it, "T1", n, hb)
                for hb in range(2):
                    if n != LEVELS[-1]:
                        use(it, "DX", n, hb)
                    use(it, "DXT", n, hb)
            for c in range(2):
                for w in ("Z", "U", "Y", "S"):
                    use(it, w, c)
        for k in range(4):
            use("mean", k)
        for k in range(4):
            use("var", k)

        @block.sync
        def _(sp):
            B = Book("sp")
            sp.dma_start(par[:, :], params).then_inc(inputs_landed, 16)
            sp.dma_start(con[:, :], consts).then_inc(inputs_landed, 16)
            sp.dma_start(post[:, :], pos).then_inc(inputs_landed, 16)
            sp.dma_start(xT[:, :, :], xT_in.rearrange("(j p) t -> p j t", p=P)).then_inc(inputs_landed, 16)

            def load(slot, src, kt=16, cols=P):
                sp.wait_ge(w_free[slot], B.up(f"w_free{slot}"))
                if B.loop is not None:
                    sp.sem_inc(spare, 1)
                dst = ring[slot][:, 0:kt * cols].rearrange("p (j n) -> p j n", j=kt)
                sp.dma_start(dst, src.rearrange("(j p) n -> p j n", p=P)).then_inc(w_landed[slot], 16)

            def columns(w, first, i, step, k):
                return w[:, bass.ds(i * step + (first + P * k), P)]

            def ada_rows(w, first):
                def body(i):
                    for s in range(4):
                        load(s, w[512 * s:512 * s + 512, bass.ds(i * 512 + first, 512)], kt=4, cols=512)
                return body

            def four(w, first):
                def body(i):
                    for s in range(4):
                        load(s, columns(w, first, i, 512, s))
                return body

            B.turns(sp, "ada0", 8, ada_rows(w_ada, 0))
            load(0, w_in[:, 3072:3200])
            load(1, w_in[:, 3200:3328])
            load(2, w_in[:, 3328:3360], cols=32)
            for k in range(8):
                load(k % 4, w_in[:, 3360 + P * k:3488 + P * k])
            B.turns(sp, "rkv", 6, four(w_in, 0))
            B.turns(sp, "ada1", 12, ada_rows(w_ada, 2 * D))
            for s in range(4):
                load(s, w_ada2[512 * s:512 * s + 512, 28 * P:32 * P], kt=4, cols=512)
            B.turns(sp, "w_out", 4, four(w_out, 0))

            def ffn(w_a, a_first, g0):
                def body(i):
                    for k in range(4):
                        load(UP_SLOT[2 * k], columns(w_up, g0 * 512, i, 512, k))
                        load(UP_SLOT[2 * k + 1], columns(w_up, g0 * 512 + 5632, i, 512, k))
                        load(ADA_SLOT[k], w_a[512 * k:512 * k + 512, bass.ds(i * 512 + a_first, 512)], kt=4, cols=512)
                    for s in range(4):
                        load(s, w_down[bass.ds(i * 512 + g0 * 512, 512), 512 * s:512 * s + 512], kt=4, cols=512)
                return body

            B.turns(sp, "ffn_a", 4, ffn(w_ada, 5 * D, 0))
            B.turns(sp, "ffn_b", 7, ffn(w_ada2, 0, 4))
            for k in range(4):
                load(k, w_in2[:, 3072 + P * k:3200 + P * k])
            load(0, w_in2[:, 3584:3648], cols=64)

            for half in range(2):
                def mla(i):
                    load(0, w_kvb[:, bass.ds(i * 512 + half * 2048, 512)], kt=4, cols=512)
                    for h in range(2):
                        if h == 0:
                            sp.wait_ge(w_free[1], B.up("w_free1"))
                            sp.sem_inc(spare, 1)
                        dst = ring[1][:, :].rearrange("p (j n) -> p j n", j=16)[:, :, 64 * h:64 * h + 64]
                        src = w_in2[:, bass.ds(i * 384 + (half * 1536 + 192 * h + P), 64)]
                        sp.dma_start(dst, src.rearrange("(j p) n -> p j n", p=P)).then_inc(w_landed[1], 16)
                    load(2, w_in2[:, bass.ds(i * 384 + half * 1536, P)])
                    load(3, w_in2[:, bass.ds(i * 384 + (half * 1536 + 192), P)])
                    load(0, w_in2[:, bass.ds(i * 256 + (3648 + half * 1024), P)])
                    load(1, w_in2[:, bass.ds(i * 256 + (3648 + half * 1024 + P), P)])
                    for s in range(2):
                        load(2 + s, w_ada2[1024 * s:1024 * s + 1024, bass.ds(i * 256 + (2 * D + half * 1024), 256)],
                             kt=8, cols=256)

                B.turns(sp, f"mla{half}", 4, mla)

                def proj(i):
                    for s in range(4):
                        load(s, w_mla[half * 1024:half * 1024 + 1024, bass.ds(i * 1024 + 256 * s, 256)], kt=8, cols=256)

                B.turns(sp, f"proj{half}", 2, proj)
            B.turns(sp, "gl", 4, four(w_in2, 15936))

            def dil(i):
                s = 0
                for g in range(3):
                    for which in (1, 0):
                        load(s % 4, w_in2[:, bass.ds(i * P + (5696 + which * 3072 + g * 1024), P)])
                        s += 1
                for g in range(3):
                    load(s % 4, w_in2[:, bass.ds(i * P + (5696 + 2 * 3072 + g * 1024), P)])
                    s += 1
                load(1, w_in2[:, bass.ds(i * P + 14912, P)])
                for k in range(2):
                    load(2 + k, w_in2[:, bass.ds(i * 256 + (17984 + P * k), P)])

            B.turns(sp, "dil", 8, dil)

            def dproj(i):
                for s in range(4):
                    load(s, w_dil[:, bass.ds(i * 1024 + 256 * s, 256)], kt=8, cols=256)

            B.turns(sp, "dproj", 2, dproj)
            B.turns(sp, "w_o", 4, four(w_o, 0))
            sp.wait_ge(gate_pe, 4)
            sp.dma_start(out.rearrange("(j p) t -> p j t", p=P), xT[:, :, :]).then_inc(out_landed, 16)
            sp.wait_ge(out_landed, 16)

        @block.gpsimd
        def _(pool):
            for k, credit in enumerate(w_free + bank_free + list(x_free.values()) + [ada_free]):
                pool.memset(small[:, 40 + k:41 + k], 0.0).then_inc(credit, 1)
            pool.wait_ge(gate_pe, 1)
            pool.memset(g2b[:, :], 0.0).then_inc(gate_pool, 1)
            pool.wait_ge(gate_pool, 1)
            pool.dma_start(w2a2[0:64, :], w2).then_inc(extra_landed, 16)
            pool.dma_start(w2a2[64:P, :], a2).then_inc(extra_landed, 16)
            pool.dma_start(g2a[:, :], g2[0:P, :]).then_inc(extra_landed, 16)
            pool.dma_start(g2b[0:32, :], g2[P:160, :]).then_inc(extra_landed, 16)
            pool.wait_ge(gate_pe, 2)
            pool.dma_start(pwt[:, :, :, :], pool_w.rearrange("g (k p) n -> p g k n", p=P)).then_inc(extra_landed, 16)
            B = Book("pool")

            def skip(slots=range(4), k=1):
                for slot in slots:
                    B.up(f"w_landed{slot}", 16 * k)

            def ada_rows(slot, acc, tmp, c_col, first, last, kt=4):
                pool.wait_ge(w_landed[slot], B.up(f"w_landed{slot}", 16))
                pool.sem_inc(pool_spare, 1)
                w = ring[slot][:, :].rearrange("p (j n) -> p j n", j=kt)
                for j in range(kt):
                    col = cact[:, c_col + j:c_col + j + 1]
                    if first and j == 0:
                        ins = pool.tensor_scalar(acc[:, :], w[:, j, :], col, None, ALU.mult)
                    else:
                        pool.tensor_scalar(tmp[:, :], w[:, j, :], col, None, ALU.mult).then_inc(pool_seq, 1)
                        pool.wait_ge(pool_seq, B.up("pool_seq"))
                        ins = pool.tensor_tensor(acc[:, :], tmp[:, :], acc[:, :], ALU.add)
                    ins.then_inc(pool_seq, 1)
                    pool.wait_ge(pool_seq, B.up("pool_seq"))
                    pool.sem_inc(pool_spare, 1)
                pool.sem_inc(w_free[slot], 1)
                if last:
                    pool.sem_inc(ada_sums, 1)

            def sums_read(n):
                pool.wait_ge(ada_full, B.up("ada_full", n))
                pool.sem_inc(pool_spare, 1)

            skip(range(4), 16)
            skip(range(3))
            pool.wait_ge(act_to_dve, 1)
            B.up("ada_full", 8 + 12)
            skip(range(4), 13)
            pool.wait_ge(gate_pe, 3)
            pool.dma_start(con[:, C_BLK:C_BLK + C_ATT], att_consts).then_inc(extra_landed, 16)
            skip(range(4), 4)

            def ffn(c_col):
                def body(i):
                    sums_read(1)
                    for k in range(4):
                        skip(UP_SLOT[2 * k:2 * k + 2])
                        ada_rows(ADA_SLOT[k], acc2, prod2, c_col + 4 * k, k == 0, k == 3)
                    skip()
                return body

            B.turns(pool, "ffn_a", 4, ffn(0))
            B.turns(pool, "ffn_b", 7, ffn(DT))
            skip()
            skip((0,))
            for half in range(2):
                def mla(i):
                    sums_read(1)
                    skip()
                    skip((1,))
                    skip((0, 1))
                    for s in range(2):
                        ada_rows(2 + s, acc3, prod3, DT + 8 * s, s == 0, s == 1, kt=8)

                B.turns(pool, f"mla{half}", 4, mla)
                skip(range(4), 2)

        @block.tensor
        def _(pe):
            B = Book("pe")

            def landed(slot, k=1):
                pe.wait_ge(w_landed[slot], B.up(f"w_landed{slot}", 16 * k))

            def skip(slot, k=1):
                B.up(f"w_landed{slot}", 16 * k)

            def x_bank(b):
                pe.wait_ge(x_free[b], B.up(f"x_free{b}"))
                return bank[b]

            def x_done(mm):
                mm.then_inc(x_full, 1)
                B.up("x_full")

            def ada_units(slots=range(4)):
                for slot in slots:
                    skip(slot)
                    B.up(f"w_free{slot}")

            def ada(*accs, n=4):
                pe.wait_ge(ada_sums, B.up("ada_sums", len(accs)))
                pe.wait_ge(ada_free, B.up("ada_free"))
                for k, acc in enumerate(accs):
                    for m in range(n):
                        mm = pe.matmul(bank[6][:, n * k + m:n * k + m + 1], acc[:, m * P:m * P + P], cc(C_ONES, 1),
                                       start=True, stop=True)
                mm.then_inc(ada_full, 1)

            def begin(slot, b):
                skip(slot)
                B.up(f"w_free{slot}")
                pe.wait_ge(w_free[slot], B.at(f"w_free{slot}") + 1)
                pe.wait_ge(bank_free[b], B.up(f"bank_free{b}"))

            def three(o, wh, wl, ah, al, first, last):
                pe.matmul(o, wh, ah, start=first, stop=False, skip_group_check=True)
                pe.matmul(o, wh, al, start=False, stop=False, skip_group_check=True)
                return pe.matmul(o, wl, ah, start=False, stop=last, skip_group_check=True)

            def w_parts(buf, kt, cols):
                return [w[buf][:, 0:kt * cols].rearrange("p (j n) -> p j n", j=kt) for w in (WH, WL)]

            def std(slot, buf, b, cols=P):
                begin(slot, b)
                wh, wl = w_parts(buf, 16, cols)
                for j in range(16):
                    mm = three(bank[b][0:cols, 0:T], wh[:, j], wl[:, j], AH[:, j, :], AL[:, j, :], j == 0, j == 15)
                mm.then_inc(unit_done, 1)

            def token_major(slot, buf, b):
                begin(slot, b)
                wh, wl = w_parts(buf, 16, P)
                for tt in range(2):
                    ts = slice(tt * P, tt * P + P)
                    for j in range(16):
                        o = bank[b][:, ts]
                        pe.matmul(o, AH[:, j, ts], wh[:, j], start=j == 0, stop=False, skip_group_check=True)
                        pe.matmul(o, AH[:, j, ts], wl[:, j], start=False, stop=False, skip_group_check=True)
                        mm = pe.matmul(o, AL[:, j, ts], wh[:, j], start=False, stop=j == 15, skip_group_check=True)
                mm.then_inc(unit_done, 1)

            def proj8(slot, buf, b):
                begin(slot, b)
                wh, wl = w_parts(buf, 8, 256)
                for m in range(2):
                    for j in range(8):
                        ms = slice(m * P, m * P + P)
                        mm = three(bank[b][:, m * T:m * T + T], wh[:, j, ms], wl[:, j, ms], BH[:, j, :], BL[:, j, :],
                                   j == 0, j == 7)
                mm.then_inc(unit_done, 1)

            def rms_sum(src, n, from_bank=None):
                o = x_bank(4)
                if from_bank is None:
                    pe.wait_ge(act_to_pe, B.up("act_to_pe"))
                else:
                    pe.wait_ge(bank_free[from_bank], B.at(f"bank_free{from_bank}") + 1)
                for j in range(n):
                    mm = pe.matmul(o[:, 0:T], cc(C_ONES), src[:, j, :], start=(j == 0), stop=(j == n - 1))
                x_done(mm)

            def four_std(i):
                for s in range(4):
                    std(s, s % 2, s)

            pe.wait_ge(inputs_landed, 64)
            rms_sum(sq, DT)
            
            def ada_turn(acc):
                def body(i):
                    ada_units()
                    ada(acc)
                return body

            B.turns(pe, "ada0", 8, ada_turn(acc0))
            pe.wait_ge(dve_to_pe, B.up("dve_to_pe"))
            std(0, 0, 0)
            std(1, 1, 1)
            std(2, 0, 2, cols=32)

            pe.wait_ge(extra_landed, 64)
            pe.wait_ge(act_to_pe, B.up("act_to_pe"))
            n = 0
            for j in range(RT):
                o = x_bank(XB[n % 3])
                js = slice(j * P, j * P + P)
                pe.matmul(o[:, 0:T], w2a2[:, js], tw[:, :], start=True, stop=True)
                x_done(pe.matmul(o[:, T:2 * T], w2a2[:, js], ta[:, :], start=True, stop=True))
                n += 1
            for j in range(0, RT, 2):
                o = x_bank(XB[n % 3])
                for m in range(2):
                    js = slice((j + m) * P, (j + m) * P + P)
                    pe.matmul(o[:, m * T:m * T + T], g2a[:, js], tg[:, :], start=True, stop=False)
                    mm = pe.matmul(o[:, m * T:m * T + T], g2b[:, js], tg2[:, :], start=False, stop=True)
                x_done(mm)
                n += 1
            for k in range(8):
                std(k % 4, k % 2, k % 4)
            B.turns(pe, "rkv", 6, four_std)
            pe.wait_ge(extra_landed, 80)
            pe.wait_ge(dve_to_pe, B.up("dve_to_pe"))
            for g in range(4):
                o = x_bank(XB[g % 3])
                for m in range(2):
                    for k in range(2):
                        mm = pe.matmul(o[:, m * T:m * T + T], pwt[:, g, k, m * P:m * P + P], zp[:, 2 * g + k, :],
                                       start=(k == 0), stop=(k == 1))
                x_done(mm)

            for b in range(4):
                pe.wait_ge(bank_free[b], B.at(f"bank_free{b}") + 1)
            for b in XB:
                pe.wait_ge(x_free[b], B.at(f"x_free{b}") + 1)

            def k_bank(*key):
                n = use_of[key]
                if n >= NK:
                    pe.wait_ge(k_free[n % NK], n // NK)
                return bank[K_BANK[n % NK]]

            def k_done(mm):
                mm.then_inc(k_full, 1)

            def in_sbuf(*key):
                n = use_of[key]
                pe.wait_ge(k_free[n % NK], n // NK + 1)

            def block_sums(name, src):
                for k in range(4):
                    o = k_bank(name, k)
                    k_done(pe.matmul(o[:, :], cc(C_BLK), src[:, 2 * k:2 * k + 2, :], start=True, stop=True))

            pe.wait_ge(act_to_pe, B.up("act_to_pe"))
            block_sums("kk", tmp1)
            B.turns(pe, "ada1", 12, ada_turn(acc1))
            ada_turn(acc1)(None)
            pe.wait_ge(dve_to_pe, B.up("dve_to_pe"))
            block_sums("bonus", tmp2)
            pe.wait_ge(dve_to_pe, B.up("dve_to_pe"))

            state = B.at("dve_to_pe")
            for it, (tt, hg) in enumerate(ITS):
                ts = slice(tt * P, tt * P + P)
                for w, src in (("B", Bt), ("K", Kt), ("V", rkv[:, 16:24, :])):
                    o = k_bank(it, "tr", w)
                    for pl in range(4):
                        mm = pe.transpose(o[:, pl * P:pl * P + P], src[:, 4 * hg + pl, ts], cc(C_ID))
                    k_done(mm)
                for hb in range(2):
                    rows = slice(64 * hb, 64 * hb + 64)
                    o = k_bank(it, "M1", hb)
                    for pl in range(4):
                        j = 4 * hg + pl
                        mm = pe.matmul(o[:, pl * P:pl * P + P], AR[rows, j, tt, 0, :], Bt[rows, j, ts],
                                       start=True, stop=True)
                    k_done(mm)
                for k in range(2):
                    for hb in range(2):
                        rows = slice(64 * hb, 64 * hb + 64)
                        for name, lhs in (("M24", Bt), ("M35", Kt)):
                            o = k_bank(it, name, hb, k)
                            for q in range(2):
                                j = 4 * hg + 2 * k + q
                                mm = pe.matmul(o[:, q * 256:q * 256 + 256], lhs[rows, j, ts], AR[rows, j, tt, :, :],
                                               start=True, stop=True)
                            k_done(mm)
                for lv, n in enumerate(LEVELS[1:]):
                    for hb in range(2):
                        if lv:
                            in_sbuf(it, "DX", LEVELS[lv], hb)
                            in_sbuf(it, "DXT", LEVELS[lv], hb)
                        else:
                            in_sbuf(it, "M1", hb)
                            in_sbuf(it, "M24", hb, 0)
                            in_sbuf(it, "M24", hb, 1)
                        o = k_bank(it, "T1", n, hb)
                        for pl in range(4):
                            mm = pe.matmul(o[:, pl * P:pl * P + P], M24[:, 4 * hb + pl, 0, :], X[hb][:, pl, :],
                                           start=True, stop=True)
                        k_done(mm)
                    for hb in range(2):
                        in_sbuf(it, "T1", n, hb)
                        if n != LEVELS[-1]:
                            o = k_bank(it, "DX", n, hb)
                            for pl in range(4):
                                mm = pe.matmul(o[:, pl * P:pl * P + P], XT[hb][:, pl, :], T1[hb][:, pl, :],
                                               start=True, stop=True)
                            k_done(mm)
                        o = k_bank(it, "DXT", n, hb)
                        for pl in range(4):
                            mm = pe.matmul(o[:, pl * P:pl * P + P], T1[hb][:, pl, :], XT[hb][:, pl, :],
                                           start=True, stop=True)
                        k_done(mm)
                for hb in range(2):
                    in_sbuf(it, "DXT", LEVELS[-1], hb)
                    for k in range(2):
                        in_sbuf(it, "M35", hb, k)
                for w in "BKV":
                    in_sbuf(it, "tr", w)
                for c in range(2):
                    cs = slice(64 * c, 64 * c + 64)
                    if c:
                        pe.wait_ge(dve_to_pe, state + 2 * it + 1)
                    elif tt:
                        pe.wait_ge(dve_to_pe, state + 2 * (it - 2) + 2)
                    o = k_bank(it, "Z", c)
                    for pl in range(4):
                        j = 4 * hg + pl
                        pe.matmul(o[:, pl * P:pl * P + P], AR[:, j, tt, 0, :], S[hg][:, pl, :],
                                  start=True, stop=False, skip_group_check=True)
                        for hb in range(2):
                            mm = pe.matmul(o[:, pl * P + 64 * hb:pl * P + 64 * hb + 64], M35[:, 4 * hb + pl, 0, :],
                                           VP[:, pl, hb, 64 * hb:64 * hb + 64], start=False, stop=hb == 1,
                                           skip_group_check=True)
                    k_done(mm)
                    in_sbuf(it, "Z", c)
                    o = k_bank(it, "U", c)
                    for pl in range(4):
                        for hb in range(2):
                            mm = pe.matmul(o[:, pl * P + 64 * hb:pl * P + 64 * hb + 64], XT[hb][:, pl, :],
                                           Z1[:, pl, 64 * hb:64 * hb + 64], start=True, stop=True)
                    k_done(mm)
                    in_sbuf(it, "U", c)
                    o = k_bank(it, "Y", c)
                    for pl in range(4):
                        j = 4 * hg + pl
                        oy = o[:, pl * 64:pl * 64 + 64]
                        pe.matmul(oy, S[hg][:, pl, :], AR[:, j, tt, 1, cs], start=True, stop=False,
                                  skip_group_check=True)
                        for hb in range(2):
                            pe.matmul(oy, UP[:, pl, hb, :], M24[:, 4 * hb + pl, 1, cs], start=False, stop=False,
                                      skip_group_check=True)
                            mm = pe.matmul(oy, VP[:, pl, hb, :], M35[:, 4 * hb + pl, 1, cs], start=False,
                                           stop=hb == 1, skip_group_check=True)
                    k_done(mm)
                    o = k_bank(it, "S", c)
                    for pl in range(4):
                        for hb in range(2):
                            pe.matmul(o[:, pl * P:pl * P + P], BZ[c][:, pl, :], UP[:, pl, hb, :], start=hb == 0,
                                      stop=False, skip_group_check=True)
                            mm = pe.matmul(o[:, pl * P:pl * P + P], KZ[c][:, pl, :], VP[:, pl, hb, :], start=False,
                                           stop=hb == 1, skip_group_check=True)
                    k_done(mm)
            pe.wait_ge(dve_to_pe, B.up("dve_to_pe", 8))
            block_sums("mean", rkv[:, 16:24, :])
            pe.wait_ge(act_to_pe, B.up("act_to_pe"))
            block_sums("var", tmp1)
            pe.wait_ge(dve_to_pe, B.up("dve_to_pe"))
            B.turns(pe, "w_out", 4, four_std)
            rms_sum(sq, DT)
            pe.wait_ge(dve_to_pe, B.up("dve_to_pe"))

            def ffn():
                def body(i):
                    for n in range(8):
                        std(UP_SLOT[n], n % 2, n % 4)
                        if n % 2:
                            ada_units((ADA_SLOT[n // 2],))
                    pe.wait_ge(dve_to_pe, B.up("dve_to_pe"))
                    for s in range(4):
                        begin(s, s)
                        o2 = x_bank(4 + s % 2)
                        wh, wl = w_parts(s % 2, 4, 512)

                        def down(m, js):
                            o, ms = bank[s] if m < 2 else o2, slice(m * P, m * P + P)
                            for j in js:
                                mm = three(o[:, m % 2 * T:m % 2 * T + T], wh[:, j, ms], wl[:, j, ms],
                                           HH[:, j, :], HL[:, j, :], j == 0 and m % 2 == 0, j == 3)
                            return mm

                        if s == 0:
                            for m in range(4):
                                down(m, range(3))
                            pe.wait_ge(dve_to_pe, B.up("dve_to_pe"))
                            for m in range(4):
                                mm = down(m, (3,))
                        else:
                            for m in range(4):
                                mm = down(m, range(4))
                        mm.then_inc(unit_done, 1)
                        if s == 0:
                            ada(acc2)
                return body

            B.turns(pe, "ffn_a", 4, ffn())
            B.turns(pe, "ffn_b", 7, ffn())
            rms_sum(sq, DT)
            rms_sum(sq, DT)
            pe.wait_ge(dve_to_pe, B.up("dve_to_pe"))
            for k in range(4):
                std(k, k % 2, k)
            begin(0, 0)
            wh, wl = w_parts(0, 16, 64)
            for j in range(16):
                mm = three(bank[0][0:64, 0:T], wh[:, j], wl[:, j], AH[:, j, :], AL[:, j, :], j == 0, j == 15)
            mm.then_inc(unit_done, 1)
            rms_sum(cksq, 4, 0)
            pe.wait_ge(dve_to_pe, B.up("dve_to_pe"))

            def turn(o, p):
                for n in range(3):
                    to = (n + 1) % 3 * P
                    mm = pe.transpose(o[:, to:to + P], p[:, n * P:n * P + P], cc(C_ID))
                return mm

            for half in range(2):
                def mla(i):
                    begin(0, 0)
                    o2 = x_bank(7)
                    wh, wl = w_parts(0, 4, 512)
                    for h in range(2):
                        ks = slice(256 * h, 256 * h + P)
                        for j in range(4):
                            three(bank[0][:, h * T:h * T + T], wh[:, j, ks], wl[:, j, ks], CKH[:, j, :], CKL[:, j, :],
                                  j == 0, j == 3)
                    for tt in range(2):
                        ts = slice(tt * P, tt * P + P)
                        for h in range(2):
                            vs = slice(256 * h + P, 256 * h + 256)
                            for j in range(4):
                                o = o2[:, tt * T + h * P:tt * T + h * P + P]
                                pe.matmul(o, CKH[:, j, ts], wh[:, j, vs], start=j == 0, stop=False,
                                          skip_group_check=True)
                                pe.matmul(o, CKH[:, j, ts], wl[:, j, vs], start=False, stop=False,
                                          skip_group_check=True)
                                mm = pe.matmul(o, CKL[:, j, ts], wh[:, j, vs], start=False, stop=j == 3,
                                               skip_group_check=True)
                    mm.then_inc(unit_done, 1)
                    skip(1)
                    std(1, 1, 1)
                    std(2, 0, 2)
                    std(3, 1, 3)
                    std(0, 0, 0)
                    pe.wait_ge(dve_to_pe, B.up("dve_to_pe"))
                    for h in range(2):
                        o = x_bank(4 + h)
                        rows = slice(64 * h, 64 * h + 64)
                        pairs = [(slice(0, T), slice(P, T), slice(0, T)), (slice(T, T + P), slice(0, P), slice(0, P))]
                        for os, qs, ks in pairs:
                            pe.matmul(o[:, os], qn[:, h, qs], ktn[:, h, ks], start=True, stop=False,
                                      skip_group_check=True)
                            mm = pe.matmul(o[:, os], qr[rows, qs], kpe[rows, ks], start=False, stop=True,
                                           skip_group_check=True)
                        x_done(mm)
                    std(1, 1, 1)
                    for h in range(2):
                        pe.wait_ge(dve_to_pe, B.up("dve_to_pe"))
                        x_done(turn(x_bank(4 + h), Pr[:, h, :]))
                    o = x_bank(7)
                    for h in range(2):
                        pe.wait_ge(x_free[4 + h], B.at(f"x_free{4 + h}") + 1)
                        oh = o[:, h * T:h * T + T]
                        pe.matmul(oh, vv[:, 0, h, :], PT[:, h, 0:T], start=True, stop=False, skip_group_check=True)
                        mm = pe.matmul(oh[:, P:T], vv[:, 1, h, :], PT[:, h, T:T + P], start=False, stop=True,
                                       skip_group_check=True)
                    x_done(mm)
                    ada_units((2, 3))
                    ada(acc3, n=2)

                B.turns(pe, f"mla{half}", 4, mla)
                pe.wait_ge(mix_ready, 4 * half + 4)

                def proj(i):
                    for s in range(4):
                        proj8(s, s % 2, s)

                B.turns(pe, f"proj{half}", 2, proj)
            B.turns(pe, "gl", 4, four_std)

            def dil(i):
                for n in range(6):
                    std(n % 4, n % 2, n % 4)
                token_major(2, 0, 2)
                token_major(3, 1, 3)
                pe.wait_ge(dve_to_pe, B.up("dve_to_pe"))
                for g in range(3):
                    o = x_bank(XB[g])
                    pe.matmul(o[:, 0:T], qd[:, g, P:T], kd[:, g, :], start=True, stop=True)
                    x_done(pe.matmul(o[:, T:T + P], qd[:, g, 0:P], kd[:, g, 0:P], start=True, stop=True))
                token_major(0, 0, 0)
                std(1, 1, 1)
                pe.wait_ge(dve_to_pe, B.up("dve_to_pe"))
                for g in range(3):
                    x_done(turn(x_bank(XB[g]), Pr[:, g, :]))
                std(2, 0, 2)
                for b in XB:
                    pe.wait_ge(x_free[b], B.at(f"x_free{b}") + 1)
                o = x_bank(4)
                for g in range(3):
                    pe.matmul(o[:, 0:T], vd[:, g, 0, :], PT[:, g, 0:T], start=g == 0, stop=False,
                              skip_group_check=True)
                    mm = pe.matmul(o[:, P:T], vd[:, g, 1, :], PT[:, g, T:T + P], start=False, stop=g == 2,
                                   skip_group_check=True)
                x_done(mm)
                std(3, 1, 3)

            B.turns(pe, "dil", 8, dil)
            pe.wait_ge(mix_ready, 8 + 8)

            def dproj(i):
                for s in range(4):
                    proj8(s, s % 2, s)

            B.turns(pe, "dproj", 2, dproj)
            pe.wait_ge(dve_to_pe, B.up("dve_to_pe"))
            B.turns(pe, "w_o", 4, four_std)
            rms_sum(sqf, DT, 3)

        @block.scalar
        def _(act):
            B = Book("act")

            def split(slot, buf, n=2048, dmas=1, fresh=False):
                act.wait_ge(w_landed[slot], B.up(f"w_landed{slot}", 16 * dmas))
                B.up("high_done")
                if fresh:
                    act.wait_ge(unit_done, B.at("high_done", 1))
                elif B.loop is not None or B.n["high_done"] > 2:
                    act.wait_ge(unit_done, B.at("high_done", 2))
                act.activation(WH[buf][:, 0:n], ring[slot][:, 0:n], ACT.Copy).then_inc(high_done, 1)

            def skip(slot, k=1):
                B.up(f"w_landed{slot}", 16 * k)

            def unit():
                act.wait_ge(unit_done, B.up("unit_done"))

            def xw():
                act.wait_ge(x_full, B.up("x_full"))

            def from_dve():
                act.wait_ge(dve_to_act, B.up("dve_to_act"))

            def rms(src, scale, s=sq, o=rstd):
                act.activation(s, src, ACT.Square).then_inc(act_to_pe, 1)
                xw()
                act.activation(o[:, :], bank[4][:, 0:T], ACT.Sqrt, bias=eps[:, 0:1], scale=scale)\
                    .then_inc(x_free[4], 1)

            def modulate(shift):
                from_dve()
                for j in range(DT):
                    ins = act.activation(hf[:, j, :], hf[:, j, :], ACT.Identity, bias=mod[:, shift + j:shift + j + 1],
                                         scale=gs[:, j:j + 1])
                ins.then_inc(act_seq, 1)
                act.wait_ge(act_seq, B.up("act_seq"))
                act.activation(AH[:, :, :], hf[:, :, :], ACT.Copy).then_inc(act_to_dve, 1)

            act.wait_ge(inputs_landed, 64)
            from_dve()
            rms(xT[:, :, :], 1.0 / D, sq[:, :, :])
            act.activation(cact[:, 0:32], par[:, 0:32], ACT.Silu).then_inc(act_to_dve, 1)
            for s in range(4):
                skip(s, 8)
            modulate(0)
            split(0, 0)
            split(1, 1)

            def copy_raw(b, rb, rows=P):
                act.wait_ge(raw_free, B.up("raw_free"))
                act.activation(raw[rb][0:rows, 16:272], bank[b][0:rows, 0:T], ACT.Copy).then_inc(bank_free[b], 1)

            unit()
            copy_raw(0, 0)
            split(2, 0, 512)
            unit()
            copy_raw(1, 1)
            unit()
            copy_raw(2, 0, 32)
            from_dve()
            act.activation(tw[0:64, :], tw[0:64, :], ACT.Tanh)
            act.activation(tg[:, :], tg[:, :], ACT.Sigmoid)
            act.activation(tg2[0:32, :], tg2[0:32, :], ACT.Sigmoid).then_inc(act_to_pe, 1)
            n = 0
            for j in range(RT):
                xw()
                b = XB[n % 3]
                act.activation(sg[:, j, :], bank[b][:, 0:T], ACT.Sigmoid, bias=pr("w0", j))
                act.activation(aa[:, j, :], bank[b][:, T:2 * T], ACT.Sigmoid, bias=pr("a0", j)).then_inc(x_free[b], 1)
                n += 1
            for j in range(0, RT, 2):
                xw()
                b = XB[n % 3]
                act.activation(gg[:, j:j + 2, :], bank[b][:, :], ACT.Copy).then_inc(x_free[b], 1)
                n += 1
            split(0, 0, fresh=True)
            for k in range(8):
                split((k + 1) % 4, (k + 1) % 2)
                unit()
                copy_raw(k % 4, k % 2)

            def rkv_body(last=False):
                def body(i):
                    for s in range(4):
                        if not (last and s == 3):
                            split((s + 1) % 4, (s + 1) % 2)
                        unit()
                        copy_raw(s, s % 2)
                return body

            B.turns(act, "rkv", 5, rkv_body())
            rkv_body(True)(5)
            B.up("x_full", 4)
            for s in range(4):
                skip(s, 13)

            def k_get(*key):
                n = use_of[key]
                act.wait_ge(k_full, n + 1)
                return bank[K_BANK[n % NK]], k_free[n % NK]

            from_dve()
            act.activation(tmp1[:, :, :], kkn[:, :, :], ACT.Square).then_inc(act_to_pe, 1)
            for k in range(4):
                o, f = k_get("kk", k)
                act.activation(ex[:, 2 * k:2 * k + 2, :], o[:, :], ACT.Sqrt).then_inc(f, 1)
            from_dve()
            act.activation(ex[:, :, :], csum[:, :, :], ACT.Exp, scale=-DECAY).then_inc(act_to_dve, 1)
            from_dve()
            act.activation(ex[:, :, :], csum[:, :, :], ACT.Exp, scale=DECAY).then_inc(act_to_dve, 1)
            from_dve()
            act.activation(ex[:, :, :], csum[:, :, :], ACT.Exp, scale=-DECAY).then_inc(act_to_dve, 1)
            from_dve()
            for it, (tt, hg) in enumerate(ITS):
                if it:
                    act.wait_ge(k_full, use_of[(it - 1, "S", 1)] + 1)
                for w, dst in (("B", BZ), ("K", KZ)):
                    o, f = k_get(it, "tr", w)
                    act.activation(dst[0][0:64, :, :], o[0:64, :], ACT.Copy)
                    act.activation(dst[1][64:P, :, :], o[64:P, :], ACT.Copy).then_inc(f, 1)
                o, f = k_get(it, "tr", "V")
                ov = o[:, :].rearrange("p (a b n) -> p a b n", a=4, b=2)
                act.activation(VP[:, :, 0, 0:64], ov[:, :, 0, :], ACT.Copy)
                act.activation(VP[:, :, 1, 64:P], ov[:, :, 1, :], ACT.Copy).then_inc(f, 1)
                for n in LEVELS[1:]:
                    for hb in range(2):
                        o, f = k_get(it, "T1", n, hb)
                        act.activation(T1[hb][:, :, :], o[:, :], ACT.Copy).then_inc(f, 1)
                for c in range(2):
                    rows = slice(64 * c, 64 * c + 64)
                    o, f = k_get(it, "U", c)
                    ov = o[:, :].rearrange("p (a b n) -> p a b n", a=4, b=2)
                    act.activation(UP[rows, :, 0, 0:64], ov[rows, :, 0, :], ACT.Copy)
                    act.activation(UP[rows, :, 1, 64:P], ov[rows, :, 1, :], ACT.Copy).then_inc(f, 1)
            act.wait_ge(k_free[use_of[("mean", 3)] % NK], use_of[("mean", 3)] // NK + 1)
            act.activation(tmp1[:, :, :], kkn[:, :, :], ACT.Square).then_inc(act_to_pe, 1)
            for k in range(4):
                o, f = k_get("var", k)
                act.activation(ex[:, 2 * k:2 * k + 2, :], o[:, :], ACT.Sqrt, bias=eps[:, 1:2], scale=1.0 / 64)\
                    .then_inc(f, 1)
            from_dve()
            act.activation(AH[:, 0:8, :], tmp2[:, :, :], ACT.Copy)
            act.activation(AH[:, 8:16, :], yp[:, :, :], ACT.Copy).then_inc(act_to_dve, 1)
            split(0, 0, fresh=True)

            def plain(nxt=4, last=False):
                def body(i):
                    for s in range(4):
                        if not (last and s == 3):
                            split((s + 1) % 4, (s + 1) % 2)
                        B.up("unit_done")
                return body

            B.turns(act, "w_out", 4, plain())
            from_dve()
            rms(xT[:, :, :], 1.0 / D, sq[:, :, :])
            modulate(3 * DT)

            def ffn(i):
                def finish():
                    from_dve()
                    act.activation(sil[:, :], sil[:, :], ACT.Silu).then_inc(act_to_dve, 1)

                def high(k):
                    from_dve()
                    act.activation(HH[:, k, :], hfu[:, :], ACT.Copy).then_inc(act_to_dve, 1)

                for n in range(8):
                    if n < 7:
                        split(UP_SLOT[n + 1], (n + 1) % 2)
                        if n % 2 == 0:
                            skip(ADA_SLOT[n // 2])
                    else:
                        split(0, 0)
                    if n % 2 and n > 1:
                        high(n // 2 - 1)
                    unit()
                    act.wait_ge(raw_free, B.up("raw_free"))
                    act.activation(rawu[n % 2][:, 2:T + 2], bank[n % 4][:, 0:T], ACT.Copy).then_inc(bank_free[n % 4], 1)
                    if n % 2 == 0 and n:
                        finish()
                finish()
                high(3)
                for s in range(4):
                    split((s + 1) % 4, (s + 1) % 2)
                    B.up("unit_done")

            B.turns(act, "ffn_a", 4, ffn)
            B.turns(act, "ffn_b", 7, ffn)
            from_dve()
            rms(xT[:, :, :], 1.0 / D, sq[:, :, :])
            from_dve()
            rms(xT[:, :, :], 1.0 / D, sq[:, :, :])
            modulate(6 * DT)
            from_dve()
            act.activation(sinM[:, :], ang[:, 0, :], ACT.Sin)
            act.activation(sinD[:, :], ang[:, 1, :], ACT.Sin)
            act.activation(cosM[:, :], tang[:, 0, :], ACT.Sin)
            act.activation(cosD[:, :], tang[:, 1, :], ACT.Sin).then_inc(act_seq, 1)
            act.wait_ge(act_seq, B.up("act_seq"))
            for k in range(4):
                split((k + 1) % 4, (k + 1) % 2, n=2048 if k < 3 else 1024)
                unit()
                act.activation(ckv[:, k, :], bank[k][:, 0:T], ACT.Copy)
                act.activation(cksq[:, k, :], bank[k][:, 0:T], ACT.Square).then_inc(bank_free[k], 1)
            unit()

            for h in range(2):
                act.activation(kpe[64 * h:64 * h + 64, :], bank[0][0:64, 0:T], ACT.Copy)
                act.activation(rsw[64 * h:64 * h + 32, :], bank[0][32:64, 0:T], ACT.Copy)
                ins = act.activation(rsw[64 * h + 32:64 * h + 64, :], bank[0][0:32, 0:T], ACT.Copy)
            ins.then_inc(bank_free[0], 1)
            xw()
            act.activation(rtm[:, :], bank[4][:, 0:T], ACT.Sqrt, bias=eps[:, 0:1], scale=1.0 / 512)\
                .then_inc(x_free[4], 1)
            from_dve()
            act.activation(CKH[:, :, :], ckv[:, :, :], ACT.Copy).then_inc(act_to_dve, 1)
            split(0, 0, fresh=True)

            for half in range(2):
                def mla(i):
                    split(1, 1, dmas=2)
                    unit()
                    act.activation(ktn[:, :, :], bank[0][:, :], ACT.Copy).then_inc(bank_free[0], 1)
                    act.activation(vv[:, :, :, :], bank[7][:, :], ACT.Copy).then_inc(x_free[7], 1)
                    split(2, 0)
                    unit()
                    act.activation(qr[:, :], bank[1][:, 0:T], ACT.Copy)
                    for r in range(0, P, 64):
                        act.activation(rsw[r:r + 32, :], bank[1][r + 32:r + 64, 0:T], ACT.Copy)
                        ins = act.activation(rsw[r + 32:r + 64, :], bank[1][r:r + 32, 0:T], ACT.Copy)
                    ins.then_inc(bank_free[1], 1)
                    split(3, 1)
                    unit()
                    act.activation(qn[:, 0, :], bank[2][:, 0:T], ACT.Copy).then_inc(bank_free[2], 1)
                    split(0, 0)
                    unit()
                    act.activation(qn[:, 1, :], bank[3][:, 0:T], ACT.Copy).then_inc(bank_free[3], 1)
                    split(1, 1)
                    unit()
                    act.activation(ez[:, 0, :], bank[0][:, 0:T], ACT.Exp, scale=-1.0).then_inc(act_to_dve, 1)
                    for h in range(2):
                        B.up("x_full")
                        from_dve()
                        act.activation(Pr[:, h, 0:T], Pr[:, h, 0:T], ACT.Exp, bias=small[:, 4 * h:4 * h + 1],
                                       accum_out=small[:, 4 * h + 2:4 * h + 3])
                        act.activation(Pr[:, h, T:384], Pr[:, h, T:384], ACT.Exp, bias=small[:, 4 * h + 1:4 * h + 2],
                                       accum_out=small[:, 4 * h + 3:4 * h + 4]).then_inc(act_to_dve, 1)
                    skip(2)
                    skip(3)
                    split(0, 0)
                    unit()
                    act.activation(ez[:, 1, :], bank[1][:, 0:T], ACT.Exp, scale=-1.0).then_inc(act_to_dve, 1)
                    for h in range(2):
                        xw()
                        act.activation(PT[:, h, :], bank[4 + h][:, 0:384], ACT.Copy).then_inc(x_free[4 + h], 1)
                    B.up("x_full")
                    from_dve()
                    act.activation(flat(BH)[:, bass.ds(i * 512, 512)], flat(af), ACT.Copy).then_inc(act_to_dve, 1)

                B.turns(act, f"mla{half}", 4, mla)
                B.turns(act, f"proj{half}", 2, plain())

            def gl(i):
                for s in range(4):
                    split((s + 1) % 4, (s + 1) % 2)
                    unit()
                    act.activation(flat(sgl)[:, bass.ds(i * 1024 + s * T, T)], bank[s][:, 0:T], ACT.Sigmoid)\
                        .then_inc(bank_free[s], 1)

            B.turns(act, "gl", 4, gl)

            def dil(i):
                for n in range(6):
                    split((n + 1) % 4, (n + 1) % 2)
                    unit()
                    dst = (kd, qd)[n % 2]
                    act.activation(dst[:, n // 2, :], bank[n % 4][:, 0:T], ACT.Copy).then_inc(bank_free[n % 4], 1)
                for g in range(3):
                    n = 6 + g
                    split((n + 1) % 4, (n + 1) % 2)
                    unit()
                    act.activation(vd[:, g, :, :], bank[n % 4][:, 0:T], ACT.Copy).then_inc(bank_free[n % 4], 1)
                    if g == 1:
                        B.up("x_full", 3)
                from_dve()
                act.activation(Pr[:, :, 0:T], Pr[:, :, 0:T], ACT.Exp, bias=small[:, 0:1], accum_out=small[:, 2:3])
                act.activation(Pr[:, :, T:384], Pr[:, :, T:384], ACT.Exp, bias=small[:, 1:2],
                               accum_out=small[:, 3:4]).then_inc(act_to_dve, 1)
                split(2, 0)
                unit()
                act.activation(ez[:, 0, :], bank[1][:, 0:T], ACT.Exp, scale=-1.0).then_inc(act_to_dve, 1)
                for g in range(3):
                    xw()
                    act.activation(PT[:, g, :], bank[XB[g]][:, 0:384], ACT.Copy).then_inc(x_free[XB[g]], 1)
                split(3, 1)
                unit()
                act.activation(flat(sgl)[:, bass.ds(i * 512, T)], bank[2][:, 0:T], ACT.Exp, scale=-1.0)\
                    .then_inc(bank_free[2], 1)
                B.up("x_full")
                from_dve()
                act.activation(flat(BH)[:, bass.ds(i * T, T)], af[:, 0, :], ACT.Copy).then_inc(act_to_dve, 1)
                split(0, 0)
                unit()
                act.activation(flat(sgl)[:, bass.ds(i * 512 + T, T)], bank[3][:, 0:T], ACT.Exp, scale=-1.0)\
                    .then_inc(bank_free[3], 1)

            B.turns(act, "dil", 8, dil)
            B.turns(act, "dproj", 2, plain())
            from_dve()
            act.activation(AH[:, :, :], Y[:, :, :], ACT.Copy).then_inc(act_to_dve, 1)

            def w_o_body(last=False):
                def body(i):
                    for s in range(4):
                        if not (last and s == 3):
                            split((s + 1) % 4, (s + 1) % 2)
                        unit()
                        js = bass.ds(i * 1024 + s * T, T)
                        act.activation(flat(oo)[:, js], bank[s][:, 0:T], ACT.Copy)
                        act.activation(flat(sqf)[:, js], bank[s][:, 0:T], ACT.Square).then_inc(bank_free[s], 1)
                return body

            B.turns(act, "w_o", 3, w_o_body())
            w_o_body(True)(3)
            xw()
            act.activation(rstf[:, :], bank[4][:, 0:T], ACT.Sqrt, bias=eps[:, 0:1], scale=1.0 / D).then_inc(x_free[4], 1)

        @block.vector
        def _(v):
            B = Book("dve")
            f32 = lambda t: t.bitcast(F32)

            def seq(ins):
                ins.then_inc(dve_seq, 1)
                v.wait_ge(dve_seq, B.up("dve_seq"))

            def low(slot, buf, n=2048, dmas=1):
                v.wait_ge(high_done, B.up("high_done"))
                B.up(f"w_landed{slot}", 16 * dmas)
                B.up(f"w_free{slot}")
                v.tensor_tensor(WL[buf][:, 0:n], ring[slot][:, 0:n], f32(WH[buf][:, 0:n]), ALU.subtract)\
                    .then_inc(w_free[slot], 1)

            def unit():
                v.wait_ge(unit_done, B.up("unit_done"))

            def xw():
                v.wait_ge(x_full, B.up("x_full"))

            def raw_tile(b):
                B.up(f"bank_free{b}")
                v.wait_ge(bank_free[b], B.at(f"bank_free{b}") + 1)

            def from_act():
                v.wait_ge(act_to_dve, B.up("act_to_dve"))

            def moved(b):
                B.up(f"x_free{b}")
                B.up("x_full")
                v.wait_ge(x_free[b], B.at(f"x_free{b}") + 1)

            def ada_rows(slot, acc, c_col, first, last, kt=4):
                v.wait_ge(w_landed[slot], B.up(f"w_landed{slot}", 16))
                w = ring[slot][:, :].rearrange("p (j n) -> p j n", j=kt)
                for j in range(kt):
                    col = cact[:, c_col + j:c_col + j + 1]
                    if first and j == 0:
                        ins = v.tensor_scalar(acc[:, :], w[:, j, :], col, None, ALU.mult)
                    else:
                        ins = v.scalar_tensor_tensor(acc[:, :], w[:, j, :], col, acc[:, :], ALU.mult, ALU.add)
                    if j < kt - 1:
                        seq(ins)
                ins.then_inc(w_free[slot], 1)
                B.up(f"w_free{slot}")
                v.wait_ge(w_free[slot], B.at(f"w_free{slot}") + 1)
                if last:
                    v.memset(small[:, 61:62], 0.0).then_inc(ada_sums, 1)

            def ada_units(slots=range(4)):
                for slot in slots:
                    B.up(f"w_landed{slot}", 16)
                    B.up(f"w_free{slot}")

            def ada_take(col, n=4):
                v.wait_ge(ada_full, B.up("ada_full"))
                v.tensor_tensor(mod[:, bass.ds(col, n)], bank[6][:, 0:n], par[:, bass.ds(col + PAR["b_ada"][0], n)],
                                ALU.add).then_inc(ada_free, 1)

            def wide(name, n, k=0):
                return pr(name, k, n).unsqueeze(2).broadcast_to([P, n, T])

            def normed(o, src, r, n=DT):
                seq(v.reciprocal(r[:, :], r[:, :]))
                seq(v.tensor_tensor(o, src, r[:, :].unsqueeze(1).broadcast_to([P, n, T]), ALU.mult))

            def modulated(gain, m_scale):
                seq(v.scalar_tensor_tensor(gs[:, :], mod[:, m_scale:m_scale + DT], 1.0, pr(gain, 0, DT), ALU.add,
                                           ALU.mult))
                v.memset(small[:, 60:61], 0.0).then_inc(dve_to_act, 1)
                from_act()
                v.tensor_tensor(AL[:, :, :], hf[:, :, :], f32(AH[:, :, :]), ALU.subtract).then_inc(dve_to_pe, 1)

            seq(v.memset(eps[:, 1:4], 64e-5))
            v.memset(eps[:, 0:1], 1e-6).then_inc(dve_to_act, 1)
            for b in range(2):
                v.memset(raw[b][:, 0:16], 0.0).then_inc(raw_free, 1)
            v.wait_ge(inputs_landed, 64)
            moved(4)
            normed(hf[:, :, :], xT[:, :, :], rstd)
            from_act()

            def ada_turn(acc, first):
                def body(i):
                    for s in range(4):
                        ada_rows(s, acc, 4 * s, s == 0, s == 3)
                    ada_take(i * 4 + first)
                return body

            B.turns(v, "ada0", 8, ada_turn(acc0, 0))
            v.wait_ge(ada_free, 8 + 1)
            modulated("norm1_g", DT)
            seq(v.memset(tw[:, :], 0.0))
            seq(v.memset(ta[:, :], 0.0))
            seq(v.memset(tg2[:, :], 0.0))
            v.memset(small[:, 61:62], 0.0).then_inc(gate_pe, 1)
            low(0, 0)
            low(1, 1)

            def shifted(b, rb, mu, rows=P):
                raw_tile(b)
                cur, prev = raw[rb][0:rows, 16:272], raw[rb][0:rows, 15:271]
                seq(v.tensor_tensor(dsh[0:rows, :], prev, cur, ALU.subtract))
                return cur, dsh[0:rows, :]

            unit_cols = PAR["mu"][0]
            cur, d = shifted(0, 0, 24)
            seq(v.scalar_tensor_tensor(tw[0:64, :], d[0:64], pr("mu", 24)[0:64], cur[0:64], ALU.mult, ALU.add))
            v.scalar_tensor_tensor(ta[64:P, :], d[64:P], pr("mu", 24)[64:P], cur[64:P], ALU.mult, ALU.add)\
                .then_inc(raw_free, 1)
            low(2, 0, 512)
            v.wait_ge(raw_free, 3)
            cur, d = shifted(1, 1, 25)
            v.scalar_tensor_tensor(tg[:, :], d, pr("mu", 25), cur, ALU.mult, ALU.add).then_inc(raw_free, 1)
            v.wait_ge(raw_free, 4)
            cur, d = shifted(2, 0, 26, 32)
            v.scalar_tensor_tensor(tg2[0:32, :], d, pr("mu", 26)[0:32], cur, ALU.mult, ALU.add).then_inc(raw_free, 1)
            v.wait_ge(raw_free, 5)
            v.memset(small[:, 62:63], 0.0).then_inc(dve_to_act, 1)
            v.wait_ge(x_full, B.up("x_full", 12))
            seq(v.memset(pa[0][:, 0:16], 0.0))
            seq(v.memset(pa[1][:, 0:16], 0.0))
            v.memset(small[:, 61:62], 0.0).then_inc(gate_pe, 1)
            for n in range(12):
                B.up(f"x_free{XB[n % 3]}")
            low(0, 0)
            for k in range(8):
                low((k + 1) % 4, (k + 1) % 2)
                raw_tile(k % 4)
                src = raw[k % 2]
                w, win, n = 1, WINDOWS[k // 2], 0
                cur = src
                while w < win:
                    seq(v.tensor_tensor(pa[n % 2][:, 16:272], cur[:, 16:272], cur[:, 16 - w:272 - w], ALU.add))
                    cur = pa[n % 2]
                    w, n = 2 * w, n + 1
                seq(v.scalar_tensor_tensor(zp[:, k, :], cur[:, 16:272], 1.0 / win, src[:, 16:272], ALU.mult,
                                           ALU.subtract))
                seq(v.tensor_tensor(dsh[:, 0:16], cur[:, 16:32], cc(C_INVC + 16 * (k // 2), 16), ALU.mult))
                v.tensor_tensor(zp[:, k, 0:16], dsh[:, 0:16], src[:, 16:32], ALU.subtract).then_inc(raw_free, 1)
                v.wait_ge(raw_free, 6 + k)

            B.n["raw_free"] = 13

            def rkv_body(last=False):
                def body(i):
                    for s in range(4):
                        if not (last and s == 3):
                            low((s + 1) % 4, (s + 1) % 2)
                        raw_tile(s)
                        cur, prev = raw[s % 2][:, 16:272], raw[s % 2][:, 15:271]
                        seq(v.tensor_tensor(dsh[:, :], prev, cur, ALU.subtract))
                        v.scalar_tensor_tensor(flat(rkv)[:, bass.ds(i * 1024 + s * T, T)], dsh[:, :],
                                               par[:, bass.ds(i * 4 + (PAR["mu"][0] + s), 1)], cur, ALU.mult,
                                               ALU.add).then_inc(raw_free, 1)
                        v.wait_ge(raw_free, B.up("raw_free"))
                return body

            B.turns(v, "rkv", 5, rkv_body())
            rkv_body(True)(5)
            v.memset(small[:, 61:62], 0.0).then_inc(dve_to_pe, 1)
            for g in range(4):
                xw()
                b = XB[g % 3]
                for m in range(2):
                    k = 2 * g + m
                    ins = v.tensor_scalar(yp[:, k, :], bank[b][:, m * T:m * T + T], pr("pool_b", k), pr("pool_s", k),
                                          ALU.add, ALU.mult)
                ins.then_inc(x_free[b], 1)
                B.up(f"x_free{b}")

            r, k_, vT = rkv[:, 0:8, :], rkv[:, 8:16, :], rkv[:, 16:24, :]

            def k_get(*key):
                n = use_of[key]
                v.wait_ge(k_full, n + 1)
                return bank[K_BANK[n % NK]], k_free[n % NK]

            def act_moved(*key):
                n = use_of[key]
                v.wait_ge(k_free[n % NK], n // NK + 1)

            v.wait_ge(unit_done, 35)
            B.n["unit_done"] = 35
            v.tensor_tensor(kkn[:, :, :], k_, wide("k_k", 8), ALU.mult).then_inc(dve_to_act, 1)
            seq(v.memset(scanm[:, :, :], 1.0))
            sm = flat(scanm).rearrange("p (n c) -> p n c", c=CH)
            seq(v.memset(sm[:, :, 0:1], 0.0))
            seq(v.scalar_tensor_tensor(csum[:, :, :], aa[:, :, :], -1.0, wide("k_a", 8), ALU.add, ALU.mult))
            seq(v.scalar_tensor_tensor(k_, csum[:, :, :], 1.0, k_, ALU.add, ALU.mult))
            seq(v.tensor_tensor(tmp2[:, :, :], r, k_, ALU.mult))
            v.tensor_tensor(tmp2[:, :, :], tmp2[:, :, :], wide("r_k", 8), ALU.mult).then_inc(dve_to_pe, 1)
            seq(v.tensor_tensor_scan(flat(csum), flat(scanm), flat(sg), 0.0, ALU.mult, ALU.add))
            for k in range(4):
                act_moved("kk", k)
            seq(v.tensor_scalar(ex[:, :, :], ex[:, :, :], 1e-12, None, ALU.max))
            seq(v.reciprocal(ex[:, :, :], ex[:, :, :]))
            v.tensor_tensor(kkn[:, :, :], kkn[:, :, :], ex[:, :, :], ALU.mult).then_inc(dve_to_act, 1)
            v.wait_ge(dve_to_act, 5)

            def tiles(t):
                return t.rearrange("p j (a n) -> p j a n", a=2)

            B.turns(v, "ada1", 12, ada_turn(acc1, 2 * DT))
            for s in range(4):
                ada_rows(s, acc1, DT + 4 * s, s == 0, s == 3)
            ada_take(7 * DT + 12)

            from_act()
            ends = flat(ex).rearrange("p (j n c) -> p j n c", j=8, c=CH)
            seq(v.tensor_copy(pc[:, :, :], ends[:, :, :, CH - 1]))
            v.tensor_tensor(AR[:, :, :, 1, :], tiles(r), tiles(ex[:, :, :]), ALU.mult).then_inc(dve_to_act, 1)
            seq(v.tensor_tensor(Bt[:, :, :], kkn[:, :, :], aa[:, :, :], ALU.mult))
            v.wait_ge(dve_to_act, 6)
            for k in range(4):
                o, f = k_get("bonus", k)
                v.tensor_tensor(bon[:, 2 * k:2 * k + 2, :], o[:, :].rearrange("p (a b) -> p a b", a=2),
                                vT[:, 2 * k:2 * k + 2, :], ALU.mult).then_inc(f, 1)
            from_act()
            seq(v.tensor_tensor(Kt[:, :, :], k_, ex[:, :, :], ALU.mult))
            seq(v.tensor_tensor(Bt[:, :, :], Bt[:, :, :], ex[:, :, :], ALU.mult))
            v.tensor_tensor(csum[:, :, :], csum[:, :, :], sg[:, :, :], ALU.subtract).then_inc(dve_to_act, 1)
            for t in (BZ[0], BZ[1], KZ[0], KZ[1], Z1, S[0], S[1]):
                seq(v.memset(t[:, :, :], 0.0))
            seq(v.memset(UP[:, :, :, :], 0.0))
            v.memset(VP[:, :, :, :], 0.0).then_inc(dve_to_act, 1)
            from_act()
            v.scalar_tensor_tensor(AR[:, :, :, 0, :], tiles(kkn[:, :, :]), -1.0, tiles(ex[:, :, :]), ALU.mult,
                                   ALU.mult).then_inc(dve_to_pe, 1)

            def many(t, n):
                return t.unsqueeze(1).broadcast_to([P, n, t.shape[-1]])

            def mask(start, n):
                return many(cc(start).bitcast(I32), n)

            v.wait_ge(dve_to_pe, 4)
            for it, (tt, hg) in enumerate(ITS):
                for hb in range(2):
                    seq(v.tensor_copy(X[hb][:, :, :], many(cc(C_ID), 4)))
                    seq(v.tensor_copy(XT[hb][:, :, :], many(cc(C_ID), 4)))
                for hb in range(2):
                    o, f = k_get(it, "M1", hb)
                    v.copy_predicated(X[hb][:, :, :], mask(C_LOW, 4), o[:, :].rearrange("p (a b) -> p a b", a=4))\
                        .then_inc(f, 1)
                for k in range(2):
                    for hb in range(2):
                        o, f = k_get(it, "M24", hb, k)
                        ov = o[:, :].rearrange("p (q m n) -> p q m n", q=2, m=2)
                        hs = slice(4 * hb + 2 * k, 4 * hb + 2 * k + 2)
                        v.tensor_tensor(M24[:, hs, :, :].rearrange("p q m n -> p q (m n)"),
                                        o[:, :].rearrange("p (q n) -> p q n", q=2), many(cc(C_MU, 256), 2), ALU.mult)
                        v.copy_predicated(XT[hb][:, 2 * k:2 * k + 2, :], mask(C_LOWT, 2), ov[:, :, 0, :])\
                            .then_inc(f, 1)
                        o, f = k_get(it, "M35", hb, k)
                        v.tensor_tensor(M35[:, hs, :, :].rearrange("p q m n -> p q (m n)"),
                                        o[:, :].rearrange("p (q n) -> p q n", q=2), many(cc(C_MU, 256), 2), ALU.mult)\
                            .then_inc(f, 1)
                for lv, n in enumerate(LEVELS[1:]):
                    for hb in range(2):
                        if n != LEVELS[-1]:
                            o, f = k_get(it, "DX", n, hb)
                            v.copy_predicated(X[hb][:, :, :], mask(C_LOW + P * (lv + 1), 4),
                                              o[:, :].rearrange("p (a b) -> p a b", a=4)).then_inc(f, 1)
                        o, f = k_get(it, "DXT", n, hb)
                        v.copy_predicated(XT[hb][:, :, :], mask(C_LOWT + P * (lv + 1), 4),
                                          o[:, :].rearrange("p (a b) -> p a b", a=4)).then_inc(f, 1)
                for c in range(2):
                    rows = slice(64 * c, 64 * c + 64)
                    n = 2 * tt + c
                    seq(v.tensor_tensor(pcbd[:, :, :], many(cc(C_BLK), 4),
                                        pc[:, 4 * hg:4 * hg + 4, n].unsqueeze(2).broadcast_to([P, 4, P]), ALU.mult))
                    o, f = k_get(it, "Z", c)
                    v.tensor_copy(Z1[rows, :, :], o[rows, :].rearrange("p (a b) -> p a b", a=4)).then_inc(f, 1)
                    o, f = k_get(it, "Y", c)
                    v.tensor_copy(rkv[:, 16 + 4 * hg:20 + 4 * hg, CH * n:CH * n + CH],
                                  o[:, 0:256].rearrange("p (a b) -> p a b", a=4)).then_inc(f, 1)
                    o, f = k_get(it, "S", c)
                    v.tensor_tensor(stmp[:, :, :], o[:, :].rearrange("p (a b) -> p a b", a=4), S[hg][:, :, :],
                                    ALU.add).then_inc(f, 1)
                    act_moved(it, "S", c)
                    v.tensor_tensor(S[hg][:, :, :], stmp[:, :, :], pcbd[:, :, :], ALU.mult).then_inc(dve_to_pe, 1)
                    v.wait_ge(dve_to_pe, 4 + 2 * it + c + 1)
            for k in range(4):
                o, f = k_get("mean", k)
                v.scalar_tensor_tensor(kkn[:, 2 * k:2 * k + 2, :], o[:, :].rearrange("p (a b) -> p a b", a=2),
                                       -1.0 / 64, vT[:, 2 * k:2 * k + 2, :], ALU.mult, ALU.add).then_inc(f, 1)
            for k in range(4):
                act_moved("mean", k)
            for k in range(4):
                act_moved("var", k)
            seq(v.reciprocal(ex[:, :, :], ex[:, :, :]))
            seq(v.tensor_tensor(kkn[:, :, :], kkn[:, :, :], ex[:, :, :], ALU.mult))
            seq(v.tensor_tensor(kkn[:, :, :], kkn[:, :, :], wide("ln_w", 8), ALU.mult))
            seq(v.tensor_tensor(kkn[:, :, :], kkn[:, :, :], wide("ln_b", 8), ALU.add))
            seq(v.tensor_tensor(kkn[:, :, :], kkn[:, :, :], bon[:, :, :], ALU.add))
            seq(v.tensor_tensor(tmp2[:, :, :], kkn[:, :, :], gg[:, :, :], ALU.mult))
            v.memset(small[:, 61:62], 0.0).then_inc(dve_to_act, 1)
            from_act()
            seq(v.tensor_tensor(AL[:, 0:8, :], tmp2[:, :, :], f32(AH[:, 0:8, :]), ALU.subtract))
            v.tensor_tensor(AL[:, 8:16, :], yp[:, :, :], f32(AH[:, 8:16, :]), ALU.subtract).then_inc(dve_to_pe, 1)
            v.memset(small[:, 61:62], 0.0).then_inc(gate_pe, 1)
            B.n["dve_to_pe"] = 13
            low(0, 0)

            def w_out_body(i):
                for s in range(4):
                    low((s + 1) % 4, (s + 1) % 2)
                    unit()
                    js = bass.ds(i * 1024 + s * T, T)
                    v.scalar_tensor_tensor(flat(xT)[:, js], bank[s][:, 0:T], mod[:, bass.ds(i * 4 + (2 * DT + s), 1)],
                                           flat(xT)[:, js], ALU.mult, ALU.add).then_inc(bank_free[s], 1)
                    B.up(f"bank_free{s}")

            B.turns(v, "w_out", 4, w_out_body)

            def taken(b):
                v.wait_ge(bank_free[b], B.at(f"bank_free{b}") + 1)

            for s in range(4):
                taken(s)
            v.memset(small[:, 61:62], 0.0).then_inc(dve_to_act, 1)
            moved(4)
            normed(hf[:, :, :], xT[:, :, :], rstd)
            v.wait_ge(ada_free, 8 + 13 + 1)
            modulated("norm2_g", 4 * DT)
            B.up("dve_to_pe")
            seq(v.memset(dacc[:, :, :], 0.0))
            for b in range(2):
                seq(v.memset(rawu[b][:, 0:2], 0.0))

            def ffn(a_first, g0):
                def body(i):
                    def conv(n):
                        raw_tile(n % 4)
                        u = rawu[n % 2]
                        gate = n % 2
                        o = sil[:, :] if gate else cva[n // 2 % 2][:, :]
                        k = n // 2
                        w = i * 12 + (PAR["conv"][0] + 12 * g0 + 3 * k + gate * 132)
                        bcol = i * 4 + (PAR["conv_b"][0] + 4 * g0 + k + gate * 44)
                        seq(v.tensor_scalar(o, u[:, 2:T + 2], par[:, bass.ds(w + 2, 1)], par[:, bass.ds(bcol, 1)],
                                            ALU.mult, ALU.add))
                        seq(v.scalar_tensor_tensor(o, u[:, 1:T + 1], par[:, bass.ds(w + 1, 1)], o, ALU.mult, ALU.add))
                        v.scalar_tensor_tensor(o, u[:, 0:T], par[:, bass.ds(w, 1)], o, ALU.mult, ALU.add)\
                            .then_inc(raw_free, 1)
                        v.wait_ge(raw_free, B.up("raw_free"))

                    def gated(k):
                        from_act()
                        seq(v.tensor_tensor(hfu[:, :], sil[:, :], cva[k % 2][:, :], ALU.mult))
                        v.memset(small[:, 61:62], 0.0).then_inc(dve_to_act, 1)

                    def low_hidden(k):
                        from_act()
                        ins = v.tensor_tensor(HL[:, k, :], hfu[:, :], f32(HH[:, k, :]), ALU.subtract)
                        if k < 2:
                            seq(ins)
                        else:
                            ins.then_inc(dve_to_pe, 1)
                            v.wait_ge(dve_to_pe, B.up("dve_to_pe"))

                    for n in range(8):
                        if n < 7:
                            low(UP_SLOT[n + 1], (n + 1) % 2)
                        else:
                            low(0, 0)
                        if n % 2 and n > 1:
                            low_hidden(n // 2 - 1)
                        conv(n)
                        if n % 2:
                            v.memset(small[:, 61:62], 0.0).then_inc(dve_to_act, 1)
                            ada_units((ADA_SLOT[n // 2],))
                        elif n:
                            gated(n // 2 - 1)
                    gated(3)
                    low_hidden(3)
                    B.up("unit_done", 8)
                    for s in range(4):
                        low((s + 1) % 4, (s + 1) % 2)
                        unit()
                        for m, o in ((0, bank[s]), (1, bank[4 + s % 2])):
                            d = dacc[:, 4 * s + 2 * m:4 * s + 2 * m + 2, :]
                            ins = v.tensor_tensor(d, o[:, :].rearrange("p (a b) -> p a b", a=2), d, ALU.add)
                            if m == 0:
                                ins.then_inc(bank_free[s], 1)
                                B.up(f"bank_free{s}")
                            else:
                                ins.then_inc(x_free[4 + s % 2], 1)
                                B.up(f"x_free{4 + s % 2}")
                        if s == 0:
                            ada_take(i * 4 + a_first)
                return body

            B.turns(v, "ffn_a", 4, ffn(5 * DT, 0))
            B.turns(v, "ffn_b", 7, ffn(6 * DT, 4))
            for s in range(4):
                taken(s)
            for b in (4, 5):
                v.wait_ge(x_free[b], B.at(f"x_free{b}") + 1)

            def along(t, n=DT):
                return t.unsqueeze(2).broadcast_to([P, n, T])

            seq(v.tensor_tensor(dacc[:, :, :], dacc[:, :, :], along(mod[:, 5 * DT:6 * DT]), ALU.mult))
            seq(v.tensor_tensor(xT[:, :, :], xT[:, :, :], dacc[:, :, :], ALU.add))
            v.memset(small[:, 61:62], 0.0).then_inc(dve_to_act, 1)
            moved(4)
            normed(xT[:, :, :], xT[:, :, :], rstd)
            seq(v.tensor_tensor(xT[:, :, :], xT[:, :, :], wide("norm_f", DT), ALU.mult))
            v.memset(small[:, 61:62], 0.0).then_inc(dve_to_act, 1)
            moved(4)
            normed(hf[:, :, :], xT[:, :, :], rstd)
            v.wait_ge(ada_free, 8 + 13 + 11 + 1)
            modulated("g_pre", 7 * DT)
            v.wait_ge(dve_to_pe, B.up("dve_to_pe"))
            seq(v.tensor_copy(posf[:, :], post[:, :]))
            INV, PI = 0.15915494309189535, 3.1415925
            C1, C2, C3 = 6.28125, 0.0019350051879882812, 3.019916e-07
            MAGIC = 12582912.0
            for k in range(2):
                a, ta_, tr = ang[:, k, :], tang[:, k, :], tred[:, k, :]
                seq(v.tensor_scalar(a, posf[:, :], pr("freq", 2 * k), None, ALU.mult))
                for o, quarter, add in ((ta_, 0.25, 1.5707964), (a, 0.0, 0.0)):
                    seq(v.tensor_scalar(tr, a, INV, quarter, ALU.mult, ALU.add))
                    seq(v.tensor_scalar(tr, tr, MAGIC, MAGIC, ALU.add, ALU.subtract))
                    seq(v.scalar_tensor_tensor(o, tr, -C1, a, ALU.mult, ALU.add))
                    seq(v.scalar_tensor_tensor(o, tr, -C2, o, ALU.mult, ALU.add))
                    seq(v.scalar_tensor_tensor(o, tr, -C3, o, ALU.mult, ALU.add))
                    seq(v.tensor_scalar(o, o, add, PI, ALU.add, ALU.min))
                    seq(v.tensor_scalar(o, o, -PI, None, ALU.max))
            v.memset(small[:, 61:62], 0.0).then_inc(dve_to_act, 1)
            for k in range(4):
                low((k + 1) % 4, (k + 1) % 2, n=2048 if k < 3 else 1024)
                raw_tile(k)
            raw_tile(0)

            def rotate(o, cos, sin, pair):
                seq(v.tensor_tensor(o, o, cos, ALU.mult))
                seq(v.tensor_tensor(pair, pair, sin, ALU.mult))
                return v.tensor_tensor(o, o, pair, ALU.add)

            seq(v.tensor_scalar(sinM[:, :], sinM[:, :], pr("freq", 1), None, ALU.mult))
            seq(v.tensor_scalar(sinD[:, :], sinD[:, :], pr("freq", 3), None, ALU.mult))
            seq(rotate(kpe[:, :], cosM[:, :], sinM[:, :], rsw[:, :]))
            moved(4)
            normed(ckv[:, :, :], ckv[:, :, :], rtm, 4)
            seq(v.tensor_tensor(ckv[:, :, :], ckv[:, :, :], wide("g_kv", 4), ALU.mult))
            v.memset(small[:, 61:62], 0.0).then_inc(dve_to_act, 1)
            from_act()
            v.tensor_tensor(CKL[:, :, :], ckv[:, :, :], f32(CKH[:, :, :]), ALU.subtract).then_inc(dve_to_pe, 1)
            low(0, 0)
            B.up("unit_done", 5)
            v.wait_ge(extra_landed, 96)

            def scored(b, p, scale, m):
                seq(v.scalar_tensor_tensor(p, bank[b][:, 0:384], scale, con[:, C_BLK + 384 * m:C_BLK + 384 * m + 384],
                                           ALU.mult, ALU.add))

            def opened(k):
                seq(v.tensor_scalar(k, k, 1.0, None, ALU.add))
                v.memset(small[:, 63:64], 0.0)
                seq(v.reciprocal(k, k))

            for half in range(2):
                def mla(i):
                    low(1, 1, dmas=2)
                    B.up("bank_free0")
                    B.up("x_free7")
                    low(2, 0)
                    raw_tile(1)
                    seq(rotate(qr[:, :], cosM[:, :], sinM[:, :], rsw[:, :]))
                    low(3, 1)
                    raw_tile(2)
                    low(0, 0)
                    raw_tile(3)
                    v.memset(small[:, 61:62], 0.0).then_inc(dve_to_pe, 1)
                    low(1, 1)
                    B.up("unit_done", 4)
                    unit()
                    from_act()
                    opened(ez[:, 0, :])
                    v.tensor_tensor(zs[:, 0, :], bank[0][:, 0:T], ez[:, 0, :], ALU.mult).then_inc(bank_free[0], 1)
                    B.up("bank_free0")
                    for h in range(2):
                        xw()
                        p = Pr[:, h, :]
                        v.scalar_tensor_tensor(p, bank[4 + h][:, 0:384], 192 ** -0.5, con[:, C_BLK:C_BLK + 384],
                                               ALU.mult, ALU.add).then_inc(x_free[4 + h], 1)
                        B.up(f"x_free{4 + h}")
                        v.wait_ge(x_free[4 + h], B.at(f"x_free{4 + h}") + 1)
                        v.tensor_reduce(small[:, 4 * h:4 * h + 1], p[:, 0:T], AX.X, ALU.max, negate=True)
                        v.tensor_reduce(small[:, 4 * h + 1:4 * h + 2], p[:, T:384], AX.X, ALU.max, negate=True)\
                            .then_inc(dve_to_act, 1)
                    for h in range(2):
                        from_act()
                        p = Pr[:, h, :]
                        seq(v.reciprocal(small[:, 4 * h + 2:4 * h + 4], small[:, 4 * h + 2:4 * h + 4]))
                        v.tensor_scalar(p[:, 0:T], p[:, 0:T], small[:, 4 * h + 2:4 * h + 3], None, ALU.mult)
                        v.tensor_scalar(p[:, T:384], p[:, T:384], small[:, 4 * h + 3:4 * h + 4], None, ALU.mult)\
                            .then_inc(dve_to_pe, 1)
                    ada_units((2, 3))
                    low(0, 0)
                    unit()
                    from_act()
                    opened(ez[:, 1, :])
                    v.tensor_tensor(zs[:, 1, :], bank[1][:, 0:T], ez[:, 1, :], ALU.mult).then_inc(bank_free[1], 1)
                    B.up("bank_free1")
                    v.wait_ge(bank_free[1], B.at("bank_free1") + 1)
                    for h in range(2):
                        B.up("x_full")
                        B.up(f"x_free{4 + h}")
                    xw()
                    v.tensor_tensor(flat(af), bank[7][:, :], flat(zs), ALU.mult).then_inc(x_free[7], 1)
                    B.up("x_free7")
                    v.wait_ge(x_free[7], B.at("x_free7") + 1)
                    v.memset(small[:, 61:62], 0.0).then_inc(dve_to_act, 1)
                    from_act()
                    o = bass.ds(i * 512, 512)
                    v.tensor_tensor(flat(BL)[:, o], flat(af), f32(flat(BH)[:, o]), ALU.subtract).then_inc(mix_ready, 1)
                    ada_take(i * 2 + (8 * DT + 8 * half), 2)

                B.turns(v, f"mla{half}", 4, mla)

                def proj(i):
                    for s in range(4):
                        low((s + 1) % 4, (s + 1) % 2)
                        unit()
                        o = flat(Y)[:, bass.ds(i * 2048 + s * 512, 512)]
                        if half == 0:
                            ins = v.tensor_copy(o, bank[s][:, :])
                        else:
                            ins = v.tensor_tensor(o, bank[s][:, :], o, ALU.add)
                        ins.then_inc(bank_free[s], 1)
                        B.up(f"bank_free{s}")

                B.turns(v, f"proj{half}", 2, proj)
            for s in range(4):
                taken(s)

            def gl(i):
                for s in range(4):
                    low((s + 1) % 4, (s + 1) % 2)
                    raw_tile(s)
                    js = bass.ds(i * 1024 + s * T, T)
                    seq(v.tensor_tensor(flat(Y)[:, js], flat(Y)[:, js], flat(sgl)[:, js], ALU.mult))

            B.turns(v, "gl", 4, gl)
            B.up("unit_done", 16)

            def dil(i):
                for n in range(6):
                    low((n + 1) % 4, (n + 1) % 2)
                    raw_tile(n % 4)
                    dst = (kd, qd)[n % 2]
                    v.memset(small[:, 63:64], 0.0)
                    seq(v.stream_shuffle(rsw[0:32, :], dst[0:32, n // 2, :], [k ^ 16 for k in range(32)]))
                    ins = rotate(dst[0:32, n // 2, :], cosD[0:32, :], sinD[0:32, :], rsw[0:32, :])
                    if n == 5:
                        ins.then_inc(dve_to_pe, 1)
                    else:
                        seq(ins)
                for g in range(3):
                    n = 6 + g
                    low((n + 1) % 4, (n + 1) % 2)
                    raw_tile(n % 4)
                    if g == 1:
                        for m in range(3):
                            xw()
                            b = XB[m]
                            v.scalar_tensor_tensor(Pr[:, m, :], bank[b][:, 0:384], 128 ** -0.5,
                                                   con[:, C_BLK + 384 * (m + 1):C_BLK + 384 * (m + 2)],
                                                   ALU.mult, ALU.add).then_inc(x_free[b], 1)
                            B.up(f"x_free{b}")
                            v.wait_ge(x_free[b], B.at(f"x_free{b}") + 1)
                        v.tensor_reduce(small[:, 0:1], Pr[:, :, 0:T], AX.XY, ALU.max, negate=True)
                        v.tensor_reduce(small[:, 1:2], Pr[:, :, T:384], AX.XY, ALU.max, negate=True)\
                            .then_inc(dve_to_act, 1)
                from_act()
                seq(v.reciprocal(small[:, 2:4], small[:, 2:4]))
                v.tensor_scalar(Pr[:, :, 0:T], Pr[:, :, 0:T], small[:, 2:3], None, ALU.mult)
                v.tensor_scalar(Pr[:, :, T:384], Pr[:, :, T:384], small[:, 3:4], None, ALU.mult)\
                    .then_inc(dve_to_pe, 1)
                low(2, 0)
                B.up("unit_done", 9)
                unit()
                from_act()
                opened(ez[:, 0, :])
                v.tensor_tensor(zs[:, 0, :], bank[1][:, 0:T], ez[:, 0, :], ALU.mult).then_inc(bank_free[1], 1)
                B.up("bank_free1")
                v.wait_ge(bank_free[1], B.at("bank_free1") + 1)
                for b in XB:
                    B.up("x_full")
                    B.up(f"x_free{b}")
                low(3, 1)
                raw_tile(2)
                opened(flat(sgl)[:, bass.ds(i * 512, T)])
                xw()
                v.tensor_tensor(af[:, 0, :], bank[4][:, 0:T], zs[:, 0, :], ALU.mult).then_inc(x_free[4], 1)
                B.up("x_free4")
                v.wait_ge(x_free[4], B.at("x_free4") + 1)
                v.memset(small[:, 61:62], 0.0).then_inc(dve_to_act, 1)
                from_act()
                o = bass.ds(i * T, T)
                v.tensor_tensor(flat(BL)[:, o], af[:, 0, :], f32(flat(BH)[:, o]), ALU.subtract).then_inc(mix_ready, 1)
                low(0, 0)
                raw_tile(3)
                opened(flat(sgl)[:, bass.ds(i * 512 + T, T)])
                B.up("unit_done", 2)

            B.turns(v, "dil", 8, dil)

            def dproj(i):
                for s in range(4):
                    low((s + 1) % 4, (s + 1) % 2)
                    unit()
                    o = bass.ds(i * 2048 + s * 512, 512)
                    v.tensor_tensor(flat(af), bank[s][:, :], flat(sgl)[:, o], ALU.mult).then_inc(bank_free[s], 1)
                    B.up(f"bank_free{s}")
                    v.wait_ge(bank_free[s], B.at(f"bank_free{s}") + 1)
                    seq(v.tensor_tensor(flat(Y)[:, o], flat(Y)[:, o], flat(af), ALU.add))

            B.turns(v, "dproj", 2, dproj)
            v.memset(small[:, 61:62], 0.0).then_inc(dve_to_act, 1)
            from_act()
            v.tensor_tensor(AL[:, :, :], Y[:, :, :], f32(AH[:, :, :]), ALU.subtract).then_inc(dve_to_pe, 1)

            def w_o_body(last=False):
                def body(i):
                    for s in range(4):
                        if not (last and s == 3):
                            low((s + 1) % 4, (s + 1) % 2)
                        raw_tile(s)
                return body

            B.turns(v, "w_o", 3, w_o_body())
            w_o_body(True)(3)
            seq(v.tensor_tensor(gs[:, :], mod[:, 8 * DT:9 * DT], pr("g_post", 0, DT), ALU.mult))
            moved(4)
            normed(oo[:, :, :], oo[:, :, :], rstf)
            seq(v.tensor_tensor(oo[:, :, :], oo[:, :, :], along(gs[:, :]), ALU.mult))
            v.tensor_tensor(xT[:, :, :], xT[:, :, :], oo[:, :, :], ALU.add).then_inc(gate_pe, 1)


def constants():
    import numpy as np

    i = np.arange(P)
    row, col = i[:, None], i[None, :]
    same = row // CH == col // CH
    con = np.zeros((P, C_WKV), np.float32)
    con[:, C_ONES:C_ONES + P] = 1
    con[:, C_ID:C_ID + P] = row == col
    con[:, C_BLK:C_BLK + P] = same
    con[:, C_MU:C_MU + P] = same & (row < col)
    con[:, C_MU + P:C_MU + 2 * P] = same & (row <= col)
    for k, n in enumerate(LEVELS):
        low = (row // (2 * n) == col // (2 * n)) & (row // n % 2 == 1) & (col // n % 2 == 0)
        con[:, C_LOW + P * k:C_LOW + P * k + P] = low
        con[:, C_LOWT + P * k:C_LOWT + P * k + P] = low.T
    for g, win in enumerate(WINDOWS):
        con[:, C_INVC + 16 * g:C_INVC + 16 * g + 16] = 1.0 / np.minimum(np.arange(1, 17), win)
    att = np.zeros((P, 4, 384), bool)
    causal = col <= row
    for m, dilation in enumerate((1, 1, 4, 16)):
        near = (row - col) % dilation == 0
        before = near & ((col >= row) if m == 1 else True)
        att[:, m, 0:P] = before
        att[:, m, P:2 * P] = causal & near
        att[:, m, 2 * P:] = causal & near
    att = np.where(att, 0.0, -1e30).astype(np.float32).reshape(P, C_ATT)
    f = np.float32
    freq = np.zeros((P, 4), np.float32)
    inv64 = f(1) / f(500000.0) ** (np.arange(0, 64, 2, dtype=f) / f(64))
    inv32 = f(1) / f(500000.0) ** (np.arange(0, 32, 2, dtype=f) / f(32))
    freq[:, 0] = inv64[i % 32]
    freq[:, 1] = np.where(i % 64 < 32, -1, 1)
    for first, sign in ((0, -1), (16, 1)):
        freq[first:first + 16, 2] = inv32
        freq[first:first + 16, 3] = sign
    return con, att, freq


def kernel(**inputs):
    import numpy as np
    import concourse.bacc as _bacc
    from concourse.bass_utils import run_bass_kernel_spmd as _run

    con, att, freq = constants()

    def columns(a):
        a = np.asarray(a).reshape(-1)
        return a.reshape(-1, P).T

    mu = np.asarray(inputs["mu_shift"]).reshape(-1)
    mu = np.concatenate([mu, np.zeros(27 * P - mu.size, np.float32)])
    cw = np.asarray(inputs["conv_w"])[0].reshape(3, 88, P).transpose(2, 1, 0).reshape(P, 264)
    par = dict(
        c=columns(inputs["c"]), c_2=columns(inputs["c_2"]),
        b_ada=np.concatenate([columns(inputs["b_ada"]), columns(inputs["b_ada_2"])], 1),
        norm1_g=columns(inputs["norm1_g"]), mu=columns(mu), w0=columns(inputs["w0"]), a0=columns(inputs["a0"]),
        k_k=columns(inputs["k_k"]), k_a=columns(inputs["k_a"]), r_k=columns(inputs["r_k"]),
        ln_w=columns(inputs["ln_x_w"]), ln_b=columns(inputs["ln_x_b"]), pool_b=columns(inputs["pool_b"]),
        pool_s=columns(inputs["pool_scale"]), norm2_g=columns(inputs["norm2_g"]), conv=cw,
        conv_b=columns(inputs["conv_b"]), norm_f=columns(inputs["norm_f_g"]), g_pre=columns(inputs["g_pre_2"]),
        g_post=columns(inputs["g_post_2"]), g_kv=columns(inputs["g_kv_2"]), freq=freq)
    params = np.ascontiguousarray(np.concatenate([par[n] for n in PAR], 1))
    pos = np.ascontiguousarray(np.broadcast_to(np.asarray(inputs["positions_2"]).reshape(1, T), (P, T)))
    arrays = dict(xT=np.ascontiguousarray(np.asarray(inputs["x"])[0].T), consts=con, att_consts=att, params=params,
                  pos=pos)
    for name, key in (("w_ada", "w_ada"), ("w_in", "w_in"), ("w2", "w2"), ("a2", "a2"), ("g2", "g2"),
                      ("pool_w", "pool_w"), ("w_out", "w_out"), ("w_up", "w_up"), ("w_down", "w_down"),
                      ("w_ada2", "w_ada_2"), ("w_in2", "w_in_2"), ("w_kvb", "w_kv_b_2"),
                      ("w_mla", "w_mla_proj_2"), ("w_dil", "w_dil_proj_2"), ("w_o", "w_o_2")):
        arrays[name] = np.asarray(inputs[key])[0]
    nc = _bacc.Bacc("TRN2", target_bir_lowering=False, num_devices=1)
    args = [nc.dram_tensor(name, a.shape, mybir.dt.from_np(a.dtype), kind="ExternalInput").ap()
            for name, a in arrays.items()]
    out = nc.dram_tensor("out", (D, T), F32, kind="ExternalOutput").ap()
    program(nc, *args, out)
    result = _run(nc, [arrays], core_ids=[0]).results[0]["out"]
    return np.ascontiguousarray(result.T)[None]
```
